# Optimizing a Trainium2 kernel written in Bass

```python
import jax, jax.numpy as jnp
from jax import lax
import numpy as np

D_MODEL = 1024
BATCH = 1
SEQ = 512
DEPTH = 2
DEC_BATCH = 1
DEC_SEQ = 512
PAST_LEN = 128

HEAD_DIM = 128
N_MEM = 256
MEM_HEADS = 4
MEM_WIDTH = MEM_HEADS * HEAD_DIM
DIL_GROUPS = ((128, 1), (512, 4), (2048, 16))
DIL_HEADS = 8
DIL_WIDTH = DIL_HEADS * HEAD_DIM
GLA_HEADS = 4
GLA_DK = D_MODEL // 2 // GLA_HEADS
GLA_DV = D_MODEL // GLA_HEADS
GLA_KW = GLA_HEADS * GLA_DK
GLA_VW = GLA_HEADS * GLA_DV
GLA_RANK = 16
GLA_TAU = 16.0
GLA_CHUNK = 64
BRANCH_A = DIL_WIDTH + MEM_WIDTH
BRANCH_B = GLA_VW + MEM_WIDTH
IN_A = 3 * len(DIL_GROUPS) * DIL_WIDTH + MEM_WIDTH + BRANCH_A
IN_B = 2 * GLA_KW + GLA_VW + 2 * GLA_RANK + MEM_WIDTH + BRANCH_B
N_A = (DEPTH + 1) // 2
N_B = DEPTH // 2
EPS = 1e-6
NEG = -1e30

kernel_name = 'hybrid_dilated_gla_memory_encoder'

F32 = jnp.float32

def rms_norm(x, g):
    xf = x.astype(F32)
    y = xf * lax.rsqrt(jnp.mean(xf * xf, axis=-1, keepdims=True) + EPS)
    return (y * g.astype(F32)).astype(x.dtype)

def alibi_slopes(dil):
    base = 2.0 ** (-8.0 * np.arange(1, DIL_HEADS + 1) / DIL_HEADS) / dil
    return jnp.asarray(base, F32)

def dilated_window_group(q, k, v, window, dil):
    Bn, S, H, E = q.shape
    C = window // (2 * dil)
    blk = C * dil
    nb = -(-S // blk)
    Sp = nb * blk
    pad = ((0, 0), (0, Sp - S), (0, 0), (0, 0))

    def split(t):
        return jnp.pad(t, pad).reshape(Bn, nb, C, dil, H, E)

    def neigh(t):
        tb = jnp.pad(split(t), ((0, 0), (1, 1), (0, 0), (0, 0), (0, 0), (0, 0)))
        return jnp.concatenate([tb[:, :-2], tb[:, 1:-1], tb[:, 2:]], axis=2)

    qb, kn, vn = split(q), neigh(k), neigh(v)
    s = jnp.einsum('bnirhe,bnjrhe->bnrhij', qb, kn).astype(F32) * (E ** -0.5)
    n = jnp.arange(nb)[:, None, None, None]
    r = jnp.arange(dil)[None, :, None, None]
    i = jnp.arange(C)[None, None, :, None]
    j = jnp.arange(3 * C)[None, None, None, :]
    delta = j - C - i
    key_pos = ((n - 1) * C + j) * dil + r
    valid = (jnp.abs(delta) <= C) & (key_pos >= 0) & (key_pos < S)
    dist = (jnp.abs(delta) * dil).astype(F32)[0, 0]
    bias = -alibi_slopes(dil)[:, None, None] * dist
    s = jnp.where(valid[None, :, :, None], s + bias[None, None, None], NEG)
    m = jnp.max(s, axis=-1, keepdims=True)
    p = jnp.exp(s - m)
    l = jnp.sum(p, axis=-1, keepdims=True)
    o = jnp.einsum('bnrhij,bnjrhe->bnirhe', (p / l).astype(v.dtype), vn)
    lse = (m + jnp.log(l))[..., 0]
    o = o.reshape(Bn, Sp, H, E)[:, :S]
    lse = lse.transpose(0, 1, 4, 2, 3).reshape(Bn, Sp, H)[:, :S]
    return o, lse

def dilated_mixer(qkv):
    Bn, S, _ = qkv.shape
    outs, lses = [], []
    for g, (w, d) in enumerate(DIL_GROUPS):
        base = 3 * g * DIL_WIDTH
        q, k, v = [qkv[..., base + c * DIL_WIDTH: base + (c + 1) * DIL_WIDTH].reshape(Bn, S, DIL_HEADS, HEAD_DIM) for c in range(3)]
        o, lse = dilated_window_group(q, k, v, w, d)
        outs.append(o)
        lses.append(lse)
    wts = jax.nn.softmax(jnp.stack(lses, 0), axis=0)
    o = jnp.sum(wts[..., None] * jnp.stack(outs, 0).astype(F32), axis=0)
    return o.reshape(Bn, S, DIL_WIDTH)

def gla_scan(q, k, v, logg, strict):
    Bn, H, N, C, dk = q.shape
    dv = v.shape[-1]
    b = jnp.cumsum(logg, axis=3)
    ii = jnp.arange(C)
    mask = (ii[None, :] < ii[:, None]) if strict else (ii[None, :] <= ii[:, None])
    mask3 = mask[:, :, None]

    def step(state, xs):
        qc, kc, vc, bc = xs
        qf, kf, vf = qc.astype(F32), kc.astype(F32), vc.astype(F32)
        o_inter = jnp.einsum('bhik,bhkv->bhiv', qf * jnp.exp(bc), state)
        diff = bc[:, :, :, None, :] - bc[:, :, None, :, :]
        decay = jnp.where(mask3, jnp.exp(jnp.where(mask3, diff, 0.0)), 0.0)
        att = jnp.einsum('bhik,bhjk,bhijk->bhij', qf, kf, decay)
        o_intra = jnp.einsum('bhij,bhjv->bhiv', att, vf)
        blast = bc[:, :, -1:, :]
        kdec = kf * jnp.exp(blast - bc)
        state = jnp.exp(blast[:, :, 0, :])[..., None] * state + jnp.einsum('bhjk,bhjv->bhkv', kdec, vf)
        return state, o_inter + o_intra

    xs = tuple(jnp.moveaxis(t, 2, 0) for t in (q, k, v, b))
    state0 = jnp.zeros((Bn, H, dk, dv), F32)
    _, o = lax.scan(step, state0, xs)
    return jnp.moveaxis(o, 0, 2)

def gla_mixer(q, k, v, lr_f, lr_b, wg_f, bg_f, wg_b, bg_b, onorm_g):
    Bn, S, _ = q.shape
    N = S // GLA_CHUNK

    def to_chunks(t, dh):
        return t.reshape(Bn, N, GLA_CHUNK, GLA_HEADS, dh).transpose(0, 3, 1, 2, 4)

    def from_chunks(t):
        return t.transpose(0, 2, 3, 1, 4).reshape(Bn, S, GLA_HEADS, -1)

    def rev(t):
        return t[:, ::-1]

    q = q * (GLA_DK ** -0.5)
    g_f = jax.nn.log_sigmoid((lr_f @ wg_f + bg_f).astype(F32)) / GLA_TAU
    g_b = jax.nn.log_sigmoid((lr_b @ wg_b + bg_b).astype(F32)) / GLA_TAU
    o_f = gla_scan(to_chunks(q, GLA_DK), to_chunks(k, GLA_DK), to_chunks(v, GLA_DV), to_chunks(g_f, GLA_DK), False)
    o_b = gla_scan(to_chunks(rev(q), GLA_DK), to_chunks(rev(k), GLA_DK), to_chunks(rev(v), GLA_DV), to_chunks(rev(g_b), GLA_DK), True)
    o = from_chunks(o_f) + rev(from_chunks(o_b))
    o = o * lax.rsqrt(jnp.mean(o * o, axis=-1, keepdims=True) + EPS) * onorm_g.astype(F32)
    return o.reshape(Bn, S, GLA_VW)

def memory_attention(q, mem_n, w_mem):
    Bn, S, _ = q.shape
    M = mem_n.shape[1]
    kv = mem_n @ w_mem
    kh = kv[..., :MEM_WIDTH].reshape(Bn, M, MEM_HEADS, HEAD_DIM)
    vh = kv[..., MEM_WIDTH:].reshape(Bn, M, MEM_HEADS, HEAD_DIM)
    qh = q.reshape(Bn, S, MEM_HEADS, HEAD_DIM)
    s = jnp.einsum('bshe,bmhe->bhsm', qh, kh).astype(F32) * (HEAD_DIM ** -0.5)
    p = jax.nn.softmax(s, axis=-1)
    o = jnp.einsum('bhsm,bmhe->bshe', p.astype(vh.dtype), vh)
    return o.reshape(Bn, S, MEM_WIDTH)

def layer_a(x, mem, ln_g, w_in, mem_ln_g, w_mem, w_out):
    h = rms_norm(x, ln_g)
    z = h @ w_in
    n_qkv = 3 * len(DIL_GROUPS) * DIL_WIDTH
    qkv = z[..., :n_qkv]
    q_mem = z[..., n_qkv:n_qkv + MEM_WIDTH]
    gate = z[..., n_qkv + MEM_WIDTH:]
    y_mix = dilated_mixer(qkv).astype(x.dtype)
    y_mem = memory_attention(q_mem, rms_norm(mem, mem_ln_g), w_mem)
    y = jnp.concatenate([y_mix, y_mem], axis=-1) * jax.nn.silu(gate)
    return x + y @ w_out

def layer_b(x, mem, ln_g, w_in, wg_f, bg_f, wg_b, bg_b, onorm_g, mem_ln_g, w_mem, w_out):
    h = rms_norm(x, ln_g)
    z = h @ w_in
    sizes = (GLA_KW, GLA_KW, GLA_VW, GLA_RANK, GLA_RANK, MEM_WIDTH, BRANCH_B)
    cuts = [int(c) for c in np.cumsum(sizes)[:-1]]
    q, k, v, lr_f, lr_b, q_mem, gate = jnp.split(z, cuts, axis=-1)
    y_mix = gla_mixer(q, k, v, lr_f, lr_b, wg_f, bg_f, wg_b, bg_b, onorm_g).astype(x.dtype)
    y_mem = memory_attention(q_mem, rms_norm(mem, mem_ln_g), w_mem)
    y = jnp.concatenate([y_mix, y_mem], axis=-1) * jax.nn.silu(gate)
    return x + y @ w_out

def trunk(x, mem, a_ln, a_win, a_mln, a_wmem, a_wout, b_ln, b_win, b_wg_f, b_bg_f, b_wg_b, b_bg_b, b_onorm, b_mln, b_wmem, b_wout, lnf):
    for i in range(DEPTH):
        j = i // 2
        if i % 2 == 0:
            x = layer_a(x, mem, a_ln[j], a_win[j], a_mln[j], a_wmem[j], a_wout[j])
        else:
            x = layer_b(x, mem, b_ln[j], b_win[j], b_wg_f[j], b_bg_f[j], b_wg_b[j], b_bg_b[j], b_onorm[j], b_mln[j], b_wmem[j], b_wout[j])
    return rms_norm(x, lnf)

def setup_inputs(seed: int = 0) -> dict:
    key = jax.random.key(seed)
    ks = jax.random.split(key, 24)

    def w(k, shape, fan_in):
        return jax.random.normal(k, shape, F32) * (fan_in ** -0.5)

    def gain(k, shape):
        return 1.0 + 0.02 * jax.random.normal(k, shape, F32)

    return {
        'x_prompt': jax.random.normal(ks[0], (BATCH, SEQ, D_MODEL), F32),
        'x_sample': jax.random.normal(ks[1], (DEC_BATCH, DEC_SEQ, D_MODEL), F32),
        'mem_prompt': jax.random.normal(ks[2], (BATCH, N_MEM, D_MODEL), F32),
        'mem_sample': jax.random.normal(ks[3], (DEC_BATCH, N_MEM, D_MODEL), F32),
        'a_ln': gain(ks[4], (N_A, D_MODEL)),
        'a_win': w(ks[5], (N_A, D_MODEL, IN_A), D_MODEL),
        'a_mln': gain(ks[6], (N_A, D_MODEL)),
        'a_wmem': w(ks[7], (N_A, D_MODEL, 2 * MEM_WIDTH), D_MODEL),
        'a_wout': w(ks[8], (N_A, BRANCH_A, D_MODEL), BRANCH_A),
        'b_ln': gain(ks[9], (N_B, D_MODEL)),
        'b_win': w(ks[10], (N_B, D_MODEL, IN_B), D_MODEL),
        'b_wg_f': w(ks[11], (N_B, GLA_RANK, GLA_KW), GLA_RANK),
        'b_bg_f': 0.1 * jax.random.normal(ks[12], (N_B, GLA_KW), F32),
        'b_wg_b': w(ks[13], (N_B, GLA_RANK, GLA_KW), GLA_RANK),
        'b_bg_b': 0.1 * jax.random.normal(ks[14], (N_B, GLA_KW), F32),
        'b_onorm': gain(ks[15], (N_B, GLA_DV)),
        'b_mln': gain(ks[16], (N_B, D_MODEL)),
        'b_wmem': w(ks[17], (N_B, D_MODEL, 2 * MEM_WIDTH), D_MODEL),
        'b_wout': w(ks[18], (N_B, BRANCH_B, D_MODEL), BRANCH_B),
        'lnf': gain(ks[19], (D_MODEL,)),
    }

def reference(x_prompt, x_sample, mem_prompt, mem_sample, a_ln, a_win, a_mln, a_wmem, a_wout, b_ln, b_win, b_wg_f, b_bg_f, b_wg_b, b_bg_b, b_onorm, b_mln, b_wmem, b_wout, lnf):
    y_prompt = trunk(x_prompt, mem_prompt, a_ln, a_win, a_mln, a_wmem, a_wout, b_ln, b_win, b_wg_f, b_bg_f, b_wg_b, b_bg_b, b_onorm, b_mln, b_wmem, b_wout, lnf)
    y_sample = trunk(x_sample, mem_sample, a_ln, a_win, a_mln, a_wmem, a_wout, b_ln, b_win, b_wg_f, b_bg_f, b_wg_b, b_bg_b, b_onorm, b_mln, b_wmem, b_wout, lnf)
    return (y_prompt, y_sample)


_drawn_inputs = setup_inputs


def setup_inputs(seed=0):
    import zlib

    import numpy as np

    out = dict(_drawn_inputs(seed))
    spreads = {}
    factors = {'a_ln': 8.0,
     'a_mln': 8.0,
     'b_ln': 3.149,
     'b_bg_f': 4.2,
     'b_bg_b': 11.96,
     'b_onorm': 55.752,
     'b_mln': 23.995,
     'lnf': 8.049}
    for name, (base, spread) in spreads.items():
        noise = np.random.default_rng([zlib.crc32(name.encode()), seed]).standard_normal(out[name].shape)
        drawn = base * np.exp(spread * noise) if base else spread * noise
        out[name] = __import__('jax').numpy.asarray(drawn.astype(out[name].dtype))
    for name, factor in factors.items():
        out[name] = (out[name] * factor).astype(out[name].dtype)
    return out
```

```python
from contextlib import ExitStack

import numpy as np

import concourse.bass as bass
from concourse import mybir

F32 = mybir.dt.float32
F32R = mybir.dt.float32r
U32 = mybir.dt.uint32
ALU = mybir.AluOpType
ACT = mybir.ActivationFunctionType
AX = mybir.AxisListType.X

P = 128
D = 1024
KC = D // P
SEQ = 512
NS = 2
TOK = NS * SEQ
NT = TOK // P
HD = 128
NMEM = 256
MT = NS * NMEM
DIL_HEADS = 8
DIL_W = DIL_HEADS * HD
NG = 3
MEM_HEADS = 4
MEM_W = MEM_HEADS * HD
RES = 4
QKV_A = 3 * NG * DIL_W
GATE_A = QKV_A + MEM_W
BRANCH = 1536
FC = BRANCH // P
GLA_HEADS = 4
GDV = 256
GDK = 128
RANK = 16
GQ, GK, GV = 0, GLA_HEADS * GDK, 2 * GLA_HEADS * GDK
GLR = GV + GLA_HEADS * GDV
GQM = GLR + 2 * RANK
GATE_B = GQM + MEM_W
TAU = 16.0
EPS = 1e-6
SCALE = float(HD) ** -0.5
KEYS = SEQ + 2 * P
LEVELS = [64, 32, 16, 8, 4, 2, 1]

DIL_C, MEM_C, GLA_C = 10, 4, 6
C_DIL = 0
C_MEM = [C_DIL + DIL_HEADS * DIL_C]
C_OUT = [C_MEM[0] + MEM_HEADS * MEM_C]
C_LR = C_OUT[0] + KC
C_GLA = C_LR + 1
C_MEM.append(C_GLA + GLA_HEADS * GLA_C)
C_OUT.append(C_MEM[1] + MEM_HEADS * MEM_C)
C_END = C_OUT[1] + KC


def need(engine, semaphore, count):
    if not isinstance(count, int) or count > 0:
        engine.wait_ge(semaphore, count)


def halves(j0, per, h, c):
    return (per // 2) * h + (j0 + c) // 2


def build(nc, A):
    with ExitStack() as top:
        def sb(name, shape, dt=F32, stack=top):
            return stack.enter_context(nc.sbuf_tensor(name, shape, dt))

        def sem(name):
            return top.enter_context(nc.semaphore(name))

        def scratch(name, shape):
            return nc.dram_tensor(name, shape, F32, kind="Internal").ap()

        top.enter_context(nc.allow_non_contiguous_dma(reason="gains and biases as columns, once"))

        xt_scratch = scratch("xt_scratch", (P, KC, TOK))
        mt_scratch = scratch("mt_scratch", (P, KC, MT))
        y_scratch = [scratch(f"y_scratch{i}", (FC, P, TOK)) for i in range(2)]

        def ps(name, n):
            return top.enter_context(nc.psum_tensor(name, [P, n], F32))

        z_ps = [ps("z_ps0", 512), ps("z_ps1", 512)]
        s_ps = ps("s_ps", 1024)
        t_ps = ps("t_ps", 1024)
        o_ps = ps("o_ps", 512)
        v_ps = ps("v_ps", 512)

        ident = sb("ident", [P, P])
        ones = sb("ones", [P, P])
        gains = sb("gains", [P, 5, KC])
        onorm = sb("onorm", [P, 2])

        w_raw = [sb(f"w_raw{i}", [P, FC, P]) for i in range(2)]
        w_hi = [sb(f"w_hi{i}", [P, FC, P], F32R) for i in range(2)]
        w_lo = [sb(f"w_lo{i}", [P, FC, P], F32R) for i in range(2)]
        ring_in = [sem("ring_in0"), sem("ring_in1")]
        hi_done, lo_done = sem("hi_done"), sem("lo_done")
        z_ready = [sem("z_ready0"), sem("z_ready1")]
        z_free = [sem("z_free0"), sem("z_free1")]
        ident_in, const_in, aux_in = sem("ident_in"), sem("const_in"), sem("aux_in")

        def w_view(w, col):
            return w.rearrange("(k p) c -> p k c", p=P)[:, :, bass.ds(col, P)]

        def w_load(sp, w, col, slot, j, nk=KC):
            need(sp, lo_done, j - 1)
            sp.dma_start(w_raw[slot][:, 0:nk, :], w_view(w, col)).then_inc(ring_in[slot], 16)

        def split_hi(act, j, j_half, slot, nk=KC):
            act.wait_ge(ring_in[slot], 16 * j_half + 16)
            need(act, z_ready[1], j - 1)
            act.activation(w_hi[slot][:, 0:nk, :], w_raw[slot][:, 0:nk, :], ACT.Copy).then_inc(hi_done, 1)

        def split_lo(dve, j, slot, nk=KC):
            dve.wait_ge(hi_done, j + 1)
            dve.tensor_tensor(w_lo[slot][:, 0:nk, :], w_raw[slot][:, 0:nk, :],
                              w_hi[slot][:, 0:nk, :].bitcast(F32), ALU.subtract).then_inc(lo_done, 1)

        def unit(pe, j, slot, s, hi, lo, width=SEQ, nk=KC):
            if s == 0:
                pe.wait_ge(lo_done, j + 1)
            need(pe, z_free[s], j)
            tok = slice(s * width, (s + 1) * width)
            for k in range(nk):
                pe.matmul(z_ps[s][:, 0:width], w_hi[slot][:, k, :], hi[:, k, tok], start=(k == 0), stop=False)
                pe.matmul(z_ps[s][:, 0:width], w_hi[slot][:, k, :], lo[:, k, tok], start=False, stop=False)
                mm = pe.matmul(z_ps[s][:, 0:width], w_lo[slot][:, k, :], hi[:, k, tok], start=False,
                               stop=(k == nk - 1))
            mm.then_inc(z_ready[s], 1)

        def gate_exp(act, s, j, eg, ge_done):
            act.wait_ge(z_ready[s], j + 1)
            act.activation(eg[:], z_ps[s][:], ACT.Exp, scale=-1.0).then_inc(ge_done, 1)

        def gate_silu(dve, s, out, n, eg, ge_done, gstep):
            dve.wait_ge(ge_done, n + 1)
            dve.tensor_scalar(eg[:], eg[:], 1.0, None, ALU.add).then_inc(gstep, 1)
            dve.wait_ge(gstep, 2 * n + 1)
            dve.reciprocal(eg[:], eg[:]).then_inc(gstep, 1)
            dve.wait_ge(gstep, 2 * n + 2)
            dve.tensor_tensor(out, z_ps[s][:], eg[:], ALU.mult).then_inc(z_free[s], 1)

        def carrier(dve):
            dve.tensor_copy(cell[1][:], cell[0][:])

        def load_and_transpose():
            with ExitStack() as st:
                rows = [sb(f"rows{i}", [P, D], stack=st) for i in range(2)]
                xt0 = sb("xt0", [P, KC, TOK], stack=st)
                mt0 = sb("mt0", [P, KC, MT], stack=st)
                sq = [sb(f"msq{i}", [P, MT], stack=st) for i in range(2)]
                msd = sb("msd", [P, MT], stack=st)
                row_in = [sem("row_in0"), sem("row_in1")]
                turned, moved = sem("rows_turned"), [sem("rows_moved0"), sem("rows_moved1")]
                stored = sem("xt_stored")
                m_sq, m_sum, m_sd, m_hat = sem("m_sq"), sem("m_sum"), sem("m_sd"), sem("m_hat")
                N = NT + MT // P
                srcs = [(A[n][0], i) for n in ("x_prompt", "x_sample") for i in range(SEQ // P)]
                srcs += [(A[n][0], i) for n in ("mem_prompt", "mem_sample") for i in range(NMEM // P)]
                block = st.enter_context(nc.Block())

                @block.sync
                def _(sp):
                    sp.dma_start(ident[:], A["c_ident"]).then_inc(ident_in, 16)
                    for t, (a, i) in enumerate(srcs):
                        need(sp, turned, t - 1)
                        sp.dma_start(rows[t % 2][:], a[i * P:(i + 1) * P, :]).then_inc(row_in[t % 2], 16)
                    w_load(sp, A["a_win"][0], 0, 0, 0)
                    for b in range(2):
                        sp.wait_ge(moved[b], N)
                    sp.dma_start(xt_scratch, xt0[:]).then_inc(stored, 16)
                    sp.wait_ge(m_hat, KC)
                    sp.dma_start(mt_scratch, mt0[:]).then_inc(stored, 16)
                    sp.wait_ge(stored, 32)

                @block.gpsimd
                def _(pool):
                    pool.memset(ones[:], 1.0).then_inc(aux_in, 1)
                    pool.memset(half_col[:], 0.5)
                    pool.memset(cell[0][:], 0.0).then_inc(aux_in, 1)
                    for i, n in enumerate(("a_ln", "a_mln", "b_ln", "b_mln", "lnf")):
                        g = A[n] if n == "lnf" else A[n][0]
                        pool.dma_start(gains[:, i, :], g.rearrange("(k p) -> p k", p=P)).then_inc(const_in, 16)
                    pool.dma_start(onorm[:], A["b_onorm"][0].rearrange("(k p) -> p k", p=P)).then_inc(const_in, 16)

                @block.tensor
                def _(pe):
                    pe.wait_ge(ident_in, 16)
                    pe.wait_ge(aux_in, 1)
                    for t in range(N):
                        pe.wait_ge(row_in[t % 2], 16 * (t // 2) + 16)
                        for b in range(2):
                            need(pe, moved[b], t - 1)
                        dst = (s_ps, t_ps)[t % 2]
                        for k in range(KC):
                            tr = pe.transpose(dst[:, k * P:(k + 1) * P], rows[t % 2][:, k * P:(k + 1) * P], ident[:])
                        tr.then_inc(turned, 1)
                    for k in range(KC):
                        pe.wait_ge(m_sq, k + 1)
                        pe.matmul(o_ps[:], ones[:], sq[k % 2][:], start=(k == 0), stop=(k == KC - 1)).then_inc(m_sum, 1)

                def evac(eng, copy, t, half):
                    eng.wait_ge(turned, t + 1)
                    src = (s_ps, t_ps)[t % 2][:, half * 512:(half + 1) * 512].rearrange("p (k i) -> p k i", k=4)
                    out = xt0[:, 4 * half:4 * half + 4, t * P:(t + 1) * P] if t < NT else \
                        mt0[:, 4 * half:4 * half + 4, (t - NT) * P:(t - NT + 1) * P]
                    copy(out, src).then_inc(moved[half], 1)

                @block.scalar
                def _(act):
                    for t in range(N):
                        evac(act, lambda o, i: act.activation(o, i, ACT.Copy), t, 0)
                    for b in range(2):
                        act.wait_ge(moved[b], N)
                    for k in range(KC):
                        need(act, m_sum, k - 1)
                        act.activation(sq[k % 2][:], mt0[:, k, :], ACT.Square).then_inc(m_sq, 1)
                    act.wait_ge(m_sum, KC)
                    act.activation(msd[:], o_ps[:], ACT.Sqrt, bias=eps_col[:], scale=1.0 / D).then_inc(m_sd, 1)

                @block.vector
                def _(dve):
                    dve.memset(eps_col[:], EPS).then_inc(eps_set, 1)
                    for t in range(N):
                        evac(dve, lambda o, i: dve.tensor_copy(o, i), t, 1)
                    dve.wait_ge(m_sd, 1)
                    dve.reciprocal(msd[:], msd[:]).then_inc(m_sd, 1)
                    dve.wait_ge(m_sd, 2)
                    for k in range(KC):
                        dve.tensor_tensor(mt0[:, k, :], mt0[:, k, :], msd[:], ALU.mult).then_inc(m_hat, 1)

        eps_col, half_col = sb("eps_col", [P, 1]), sb("half_col", [P, 1])
        cell = [sb("cell0", [P, 1]), sb("cell1", [P, 1])]
        eps_set = sem("eps_set")

        def norm_split(tag, xT, gain, hi, lo, permuted, first_chunk, st, load_x=False):
            sq = [sb(f"{tag}_sq{i}", [P, SEQ], stack=st) for i in range(2)]
            rstd = sb(f"{tag}_rstd", [P, TOK], stack=st)
            h = [sb(f"{tag}_h{i}", [P, SEQ], stack=st) for i in range(2)]
            sq_done, sum_done, sd_done = sem(f"{tag}_sq_done"), sem(f"{tag}_sum_done"), sem(f"{tag}_sd_done")
            r_done, h_done, hh_done, hl_done = (sem(f"{tag}_{n}") for n in ("r_done", "h_done", "hh_done", "hl_done"))
            x_in = sem(f"{tag}_x_in")
            block = st.enter_context(nc.Block())
            banks = (o_ps, v_ps)

            @block.sync
            def _(sp):
                if load_x:
                    sp.dma_start(xT[:], xt_scratch).then_inc(x_in, 16)

            @block.scalar
            def _(act):
                if load_x:
                    act.wait_ge(x_in, 16)
                act.wait_ge(eps_set, 1)
                for s in range(NS):
                    for k in range(KC):
                        n = KC * s + k
                        need(act, sum_done, n - 1)
                        act.activation(sq[n % 2][:], xT[:, k, s * SEQ:(s + 1) * SEQ], ACT.Square).then_inc(sq_done, 1)
                for s in range(NS):
                    act.wait_ge(sum_done, KC * s + KC)
                    act.activation(rstd[:, s * SEQ:(s + 1) * SEQ], banks[s][:], ACT.Sqrt, bias=eps_col[:],
                                   scale=1.0 / D).then_inc(sd_done, 1)
                for n in range(NS * KC):
                    k, s = n // NS, n % NS
                    act.wait_ge(h_done, n + 1)
                    act.activation(hi[:, k, s * SEQ:(s + 1) * SEQ], h[n % 2][:], ACT.Copy).then_inc(hh_done, 1)
                split_hi(act, first_chunk, first_chunk // 2, first_chunk % 2)

            @block.tensor
            def _(pe):
                for s in range(NS):
                    for k in range(KC):
                        pe.wait_ge(sq_done, KC * s + k + 1)
                        pe.matmul(banks[s][:], ones[:], sq[(KC * s + k) % 2][:], start=(k == 0),
                                  stop=(k == KC - 1)).then_inc(sum_done, 1)

            @block.vector
            def _(dve):
                dve.wait_ge(const_in, 16 * 6)
                if load_x:
                    dve.wait_ge(x_in, 16)
                for s in range(NS):
                    dve.wait_ge(sd_done, s + 1)
                    dve.reciprocal(rstd[:, s * SEQ:(s + 1) * SEQ], rstd[:, s * SEQ:(s + 1) * SEQ]).then_inc(r_done, 1)
                dve.wait_ge(r_done, NS)
                for n in range(NS * KC):
                    k, s = n // NS, n % NS
                    need(dve, hl_done, n - 1)
                    tok = slice(s * SEQ, (s + 1) * SEQ)
                    out, x, r = h[n % 2][:], xT[:, k, tok], rstd[:, tok]
                    if permuted:
                        out = out.rearrange("p (r i) -> p i r", r=RES)
                        x, r = (a.rearrange("p (i r) -> p i r", r=RES) for a in (x, r))
                    dve.scalar_tensor_tensor(out=out, in0=x, scalar=gains[:, gain, k:k + 1], in1=r,
                                             op0=ALU.mult, op1=ALU.mult).then_inc(h_done, 1)
                split_lo(dve, first_chunk, first_chunk % 2)

            @block.gpsimd
            def _(pool):
                for n in range(NS * KC):
                    k, s = n // NS, n % NS
                    pool.wait_ge(hh_done, n + 1)
                    pool.tensor_tensor(lo[:, k, s * SEQ:(s + 1) * SEQ], h[n % 2][:],
                                       hi[:, k, s * SEQ:(s + 1) * SEQ].bitcast(F32), ALU.subtract).then_inc(hl_done, 1)

        def dilated(hi, lo):
            with ExitStack() as st:
                qk = sb("qk", [P, 2 * NG, TOK], stack=st)
                vT = sb("vT", [P, TOK], stack=st)
                v = sb("v", [P, NG, NT, HD], stack=st)
                bias = sb("bias", [P, RES, KEYS], stack=st)
                x = [sb(f"x{i}", [P, KEYS], stack=st) for i in range(2)]
                pT = [sb(f"pT{i}", [P, 6, SEQ], stack=st) for i in range(NS)]
                gate = sb("gate", [P, TOK], stack=st)
                eg = sb("eg", [P, SEQ], stack=st)
                y = sb("y", [P, TOK], stack=st)
                mx, nm, l, rl = (sb(n, [P, 2], stack=st) for n in ("mx", "nm", "l", "rl"))
                (bias_in, bias_ready, qk_done, max_done, neg_done, exp_done, rl_done, p_ready, tr_done, pt_ready,
                 vtr_done, v_ready, pv_done, y_done, y_stored, ge_done, gstep) = (sem("dil_" + n) for n in (
                     "bias_in", "bias_ready", "qk_done", "max_done", "neg_done", "exp_done", "rl_done", "p_ready",
                     "tr_done", "pt_ready", "vtr_done", "v_ready", "pv_done", "y_done", "y_stored", "ge_done", "gstep"))
                w = A["a_win"][0]
                TPS = SEQ // P
                V0, G = 2 * NG, DIL_C - 1
                QK0 = 2 * V0
                block = st.enter_context(nc.Block())

                def col(h, c):
                    if c < V0:
                        return 3 * (c // 2) * DIL_W + (c % 2) * DIL_W + h * HD
                    if c < G:
                        return 3 * (c - V0) * DIL_W + 2 * DIL_W + h * HD
                    return GATE_A + h * HD

                @block.sync
                def _(sp):
                    def head(h, start=0, stop=DIL_C):
                        for c in range(start, stop):
                            w_load(sp, w, col(h, c), c % 2, C_DIL + DIL_C * h + c)
                    sp.dma_start(bias[:], A["c_bias"]).then_inc(bias_in, 16)
                    head(0, start=1)
                    with sp.Fori(1, DIL_HEADS) as h:
                        head(h)
                    w_load(sp, A["a_wmem"][0], 0, C_MEM[0] % 2, C_MEM[0])

                @block.gpsimd
                def _(pool):
                    def head(h, more):
                        if more:
                            pool.wait_ge(max_done, NT * h + NT)
                            pool.tensor_tensor(bias[:].rearrange("p r k -> p (r k)"), bias[:].rearrange("p r k -> p (r k)"),
                                               half_col[:].to_broadcast([P, RES * KEYS]), ALU.mult).then_inc(bias_ready, 1)
                        pool.wait_ge(y_done, NS * h + NS)
                        pool.dma_start(y_scratch[0][h], y[:]).then_inc(y_stored, 16)
                    head(0, True)
                    with pool.Fori(1, DIL_HEADS - 1) as h:
                        head(h, True)
                    head(DIL_HEADS - 1, False)
                    pool.wait_ge(y_stored, 16 * DIL_HEADS)

                @block.tensor
                def _(pe):
                    def scores(h, t):
                        s, r = t // TPS, t % TPS
                        T = NT * h + t
                        need(pe, max_done, T)
                        if t == 0:
                            need(pe, y_done, NS * h)
                            pe.wait_ge(z_free[1], C_DIL + DIL_C * h + V0)
                            pe.wait_ge(z_free[0], C_DIL + DIL_C * h + V0)
                        q = slice(s * SEQ + r * P, s * SEQ + (r + 1) * P)
                        pe.matmul(s_ps[:, 0:SEQ], qk[:, 0, q], qk[:, 1, s * SEQ:(s + 1) * SEQ], start=True, stop=True)
                        pe.matmul(s_ps[:, SEQ:SEQ + P], qk[:, 2, q], qk[:, 3, q], start=True, stop=True)
                        pe.matmul(s_ps[:, SEQ + P:KEYS], qk[:, 4, q], qk[:, 5, q], start=True, stop=True).then_inc(qk_done, 1)

                    def turn_probs(h, t):
                        T = NT * h + t
                        pe.wait_ge(p_ready, T + 1)
                        need(pe, pt_ready, T)
                        for c in range(KEYS // P):
                            tr = pe.transpose(t_ps[:, c * P:(c + 1) * P], x[t % 2][:, c * P:(c + 1) * P], ident[:])
                        tr.then_inc(tr_done, 1)

                    def turn_values(h, g, s):
                        n = NG * NS * h + NS * g + s
                        pe.wait_ge(z_free[s], C_DIL + DIL_C * h + V0 + g + 1)
                        need(pe, v_ready, n)
                        for i in range(TPS):
                            tr = pe.transpose(v_ps[:, i * P:(i + 1) * P],
                                              vT[:, s * SEQ + i * P:s * SEQ + (i + 1) * P], ident[:])
                        tr.then_inc(vtr_done, 1)

                    def weighted_values(h, s):
                        pe.wait_ge(pt_ready, NT * h + TPS * (s + 1))
                        pe.wait_ge(v_ready, NG * NS * (h + 1))
                        if s == 1:
                            pe.wait_ge(y_done, NS * h + 1)
                        for kt in range(TPS):
                            pe.matmul(o_ps[:], v[:, 0, s * TPS + kt, :], pT[s][:, kt, :], start=(kt == 0), stop=False,
                                      skip_group_check=True)
                        for r in range(TPS):
                            for g in (1, 2):
                                mm = pe.matmul(o_ps[:, r * P:(r + 1) * P], v[:, g, s * TPS + r, :],
                                               pT[s][:, TPS - 1 + g, r * P:(r + 1) * P], start=False,
                                               stop=(r == TPS - 1 and g == 2), skip_group_check=True)
                        mm.then_inc(pv_done, 1)

                    def rest(h, n):
                        if n in (0, 1):
                            turn_probs(h, NT - 2 + n)
                        if n == 0:
                            weighted_values(h, 0)
                        if n == 3:
                            weighted_values(h, 1)

                    def head(h, before):
                        for n in range(2 * DIL_C):
                            unit(pe, C_DIL + DIL_C * h + n // 2, (n // 2) % 2, n % 2, hi, lo)
                            if before is not None:
                                rest(before, n)
                            if 0 <= n - 2 * V0 - 1 < NG * NS:
                                turn_values(h, (n - 2 * V0 - 1) // 2, (n - 2 * V0 - 1) % 2)
                            if n >= QK0:
                                scores(h, n - QK0)
                            if n >= QK0 + 2:
                                turn_probs(h, n - QK0 - 2)
                    head(0, None)
                    with pe.Fori(1, DIL_HEADS) as h:
                        head(h, h - 1)
                    for n in range(4):
                        rest(DIL_HEADS - 1, n)

                @block.scalar
                def _(act):
                    def exps(h, t):
                        T = NT * h + t
                        act.wait_ge(neg_done, T + 1)
                        act.activation(x[t % 2][:], x[t % 2][:], ACT.Exp, bias=nm[:, t % 2:t % 2 + 1],
                                       accum_out=l[:, t % 2:t % 2 + 1]).then_inc(exp_done, 1)

                    def move_probs(h, t):
                        s, r = t // TPS, t % TPS
                        act.wait_ge(tr_done, NT * h + t + 1)
                        if t == 0:
                            need(act, pv_done, NS * h)
                        act.activation(pT[s][:, :, r * P:(r + 1) * P],
                                       t_ps[:, 0:KEYS].rearrange("p (c q) -> p c q", q=P), ACT.Copy).then_inc(pt_ready, 1)

                    def move(h, n):
                        c, s = n // 2, n % 2
                        j = C_DIL + DIL_C * h + c
                        tok = slice(s * SEQ, (s + 1) * SEQ)
                        if c == G:
                            gate_exp(act, s, j, eg, ge_done) if s == 0 else gate_exp2(h, j)
                            return
                        act.wait_ge(z_ready[s], j + 1)
                        if n == 0:
                            need(act, qk_done, NT * h)
                        if c >= V0:
                            need(act, vtr_done, NG * NS * h + NS * (c - V0) + s - 1)
                        out = qk[:, c, tok] if c < V0 else vT[:, tok]
                        act.activation(out, z_ps[s][:], ACT.Copy).then_inc(z_free[s], 1)

                    def gate_exp2(h, j):
                        act.wait_ge(z_free[0], j + 1)
                        gate_exp(act, 1, j, eg, ge_done)

                    def rest(h, n):
                        if n == 0:
                            move_probs(h, NT - 3)
                            exps(h, NT - 1)
                        if n in (1, 2):
                            move_probs(h, NT - 3 + n)

                    def head(h, before):
                        for n in range(2 * DIL_C):
                            c = n // 2
                            if n % 2 == 0:
                                j = C_DIL + DIL_C * h + c + 1
                                split_hi(act, j, halves(C_DIL, DIL_C, h, c + 1), (c + 1) % 2)
                            if before is not None:
                                rest(before, n)
                            if n >= QK0 + 1:
                                exps(h, n - QK0 - 1)
                            if n >= QK0 + 3:
                                move_probs(h, n - QK0 - 3)
                            move(h, n)
                    act.preload_act_table(ACT.Exp)
                    head(0, None)
                    with act.Fori(1, DIL_HEADS) as h:
                        head(h, h - 1)
                    for n in range(3):
                        rest(DIL_HEADS - 1, n)

                @block.vector
                def _(dve):
                    def softmax_in(h, t):
                        T = NT * h + t
                        b = t % 2
                        dve.wait_ge(qk_done, T + 1)
                        need(dve, tr_done, T - 1)
                        if t == 0:
                            dve.wait_ge(bias_in, 16)
                            need(dve, bias_ready, h)
                        carrier(dve)
                        dve.tensor_tensor_reduce(x[b][:], s_ps[:, 0:KEYS], bias[:, t % TPS, :], SCALE, -3e38,
                                                 ALU.add, ALU.max, mx[:, b:b + 1]).then_inc(max_done, 1)
                        dve.wait_ge(max_done, T + 1)
                        dve.tensor_scalar(nm[:, b:b + 1], mx[:, b:b + 1], -1.0, None, ALU.mult).then_inc(neg_done, 1)

                    def softmax_out(h, t):
                        T = NT * h + t
                        b = t % 2
                        dve.wait_ge(exp_done, T + 1)
                        dve.reciprocal(rl[:, b:b + 1], l[:, b:b + 1]).then_inc(rl_done, 1)
                        dve.wait_ge(rl_done, T + 1)
                        dve.tensor_scalar(x[b][:], x[b][:], rl[:, b:b + 1], None, ALU.mult).then_inc(p_ready, 1)

                    def move_values(h, m):
                        n = NG * NS * h + m
                        g, s = m // NS, m % NS
                        dve.wait_ge(vtr_done, n + 1)
                        if m == 0:
                            need(dve, pv_done, NS * h)
                        dve.tensor_copy(v[:, g, s * TPS:(s + 1) * TPS, :],
                                        v_ps[:].rearrange("p (t e) -> p t e", e=HD)).then_inc(v_ready, 1)

                    def finish(h, s):
                        dve.wait_ge(pv_done, NS * h + s + 1)
                        tok = slice(s * SEQ, (s + 1) * SEQ)
                        dve.tensor_tensor(y[:, tok].rearrange("p (i r) -> p r i", r=RES),
                                          o_ps[:].rearrange("p (r i) -> p r i", r=RES),
                                          gate[:, tok].rearrange("p (r i) -> p r i", r=RES), ALU.mult).then_inc(y_done, 1)

                    def rest(h, n):
                        if n == 0:
                            softmax_out(h, NT - 1)
                        if n == 1:
                            finish(h, 0)
                        if n == 4:
                            finish(h, 1)

                    def head(h, before):
                        for n in range(2 * DIL_C):
                            c = n // 2
                            if n % 2 == 0:
                                split_lo(dve, C_DIL + DIL_C * h + c + 1, (c + 1) % 2)
                            if before is not None and n == 0:
                                softmax_in(before, NT - 1)
                            if n >= QK0 + 1:
                                softmax_in(h, n - QK0 - 1)
                            if 0 <= n - 2 * V0 - 2 < NG * NS:
                                move_values(h, n - 2 * V0 - 2)
                            if n >= QK0 + 1:
                                softmax_out(h, n - QK0 - 1)
                            if before is not None:
                                rest(before, n)
                            if c == G:
                                if n % 2 == 0:
                                    need(dve, y_done, NS * h)
                                    need(dve, y_stored, 16 * h)
                                s = n % 2
                                gate_silu(dve, s, gate[:, s * SEQ:(s + 1) * SEQ], NS * h + s, eg, ge_done, gstep)
                    head(0, None)
                    with dve.Fori(1, DIL_HEADS) as h:
                        head(h, h - 1)
                    softmax_in(DIL_HEADS - 1, NT - 1)
                    for n in range(5):
                        rest(DIL_HEADS - 1, n)

        def memory(i, hi, lo):
            tag = "ab"[i]
            with ExitStack() as st:
                m_hat = sb(tag + "m_hat", [P, KC, MT], stack=st)
                m_g = [sb(f"{tag}m_g{b}", [P, MT], stack=st) for b in range(2)]
                m_hi = sb(tag + "m_hi", [P, KC, MT], F32R, stack=st)
                m_lo = sb(tag + "m_lo", [P, KC, MT], F32R, stack=st)
                kT = sb(tag + "kT", [P, MT], stack=st)
                vT = sb(tag + "vmT", [P, MT], stack=st)
                v = sb(tag + "vm", [P, MT // P, HD], stack=st)
                q = sb(tag + "qm", [P, TOK], stack=st)
                gate = sb(tag + "gm", [P, TOK], stack=st)
                eg = sb(tag + "egm", [P, SEQ], stack=st)
                y = sb(tag + "ym", [P, TOK], stack=st)
                p = [sb(f"{tag}pm{b}", [P, 2, NMEM], stack=st) for b in range(2)]
                pT = [sb(f"{tag}pmT{s}", [P, 2, SEQ], stack=st) for s in range(NS)]
                mx, nm, l, rl = (sb(tag + n, [P, 2, 2], stack=st) for n in ("mxm", "nmm", "lm", "rlm"))
                (mh_in, mg_done, mh_done, ml_done, qk_done, max_done, neg_done, exp_done, rl_done, p_ready, tr_done,
                 pt_ready, vtr_done, v_ready, pv_done, y_done, y_stored, ge_done, gstep) = (sem(f"{tag}mem_" + n) for n in (
                     "mh_in", "mg_done", "mh_done", "ml_done", "qk_done", "max_done", "neg_done", "exp_done", "rl_done",
                     "p_ready", "tr_done", "pt_ready", "vtr_done", "v_ready", "pv_done", "y_done", "y_stored",
                     "ge_done", "gstep"))
                wm, w = A["ab"[i] + "_wmem"][0], A["ab"[i] + "_win"][0]
                q_col = QKV_A if i == 0 else GQM
                gate_col = (GATE_A if i == 0 else GATE_B) + (BRANCH - MEM_W)
                C0 = C_MEM[i]
                NP = 4
                K, V, Q, G = range(MEM_C)
                nxt = (A["a_wout"][0], FC) if i == 0 else (A["b_wout"][0], FC)
                block = st.enter_context(nc.Block())

                @block.sync
                def _(sp):
                    sp.dma_start(m_hat[:], mt_scratch).then_inc(mh_in, 16)

                    def head(h, start=0):
                        cols = [(wm, h * HD), (wm, MEM_W + h * HD), (w, q_col + h * HD), (w, gate_col + h * HD)]
                        for c in range(start, MEM_C):
                            w_load(sp, *cols[c], (C0 + c) % 2, C0 + MEM_C * h + c)
                    head(0, start=1)
                    with sp.Fori(1, MEM_HEADS) as h:
                        head(h)
                    w_load(sp, nxt[0], 0, C_OUT[i] % 2, C_OUT[i], nk=FC)

                @block.gpsimd
                def _(pool):
                    def head(h):
                        pool.wait_ge(y_done, NS * h + NS)
                        pool.dma_start(y_scratch[i][h + (FC - MEM_HEADS)], y[:]).then_inc(y_stored, 16)
                    head(0)
                    with pool.Fori(1, MEM_HEADS) as h:
                        head(h)
                    pool.wait_ge(y_stored, 16 * MEM_HEADS)

                @block.tensor
                def _(pe):
                    def scores(h, p_):
                        N = NP * h + p_
                        need(pe, exp_done, 2 * N - 2)
                        if p_ == 0:
                            need(pe, y_done, NS * h)
                        pe.wait_ge(z_free[p_ // 2], C0 + MEM_C * h + Q + 1)
                        s = p_ // 2
                        for t in range(2):
                            tok = s * SEQ + (2 * (p_ % 2) + t) * P
                            mm = pe.matmul(s_ps[:, (p_ % 2) * 512 + t * NMEM:(p_ % 2) * 512 + (t + 1) * NMEM],
                                           q[:, tok:tok + P], kT[:, s * NMEM:(s + 1) * NMEM], start=True, stop=True)
                        mm.then_inc(qk_done, 1)

                    def turn_probs(h, p_):
                        N = NP * h + p_
                        pe.wait_ge(p_ready, 2 * N + 2)
                        need(pe, pt_ready, N - 1)
                        for m in range(2):
                            for t in range(2):
                                o = (p_ % 2) * 512 + m * 256 + t * P
                                tr = pe.transpose(t_ps[:, o:o + P], p[p_ % 2][:, t, m * P:(m + 1) * P], ident[:])
                        tr.then_inc(tr_done, 1)

                    def turn_values(h):
                        pe.wait_ge(z_free[0], C0 + MEM_C * h + V + 1)
                        pe.wait_ge(z_free[1], C0 + MEM_C * h + V + 1)
                        for m in range(MT // P):
                            tr = pe.transpose(v_ps[:, m * P:(m + 1) * P], vT[:, m * P:(m + 1) * P], ident[:])
                        tr.then_inc(vtr_done, 1)

                    def weighted_values(h, s):
                        pe.wait_ge(pt_ready, NP * h + 2 * s + 2)
                        pe.wait_ge(v_ready, h + 1)
                        if s == 1:
                            pe.wait_ge(y_done, NS * h + 1)
                        for m in range(2):
                            mm = pe.matmul(o_ps[:], v[:, 2 * s + m, :], pT[s][:, m, :], start=(m == 0), stop=(m == 1))
                        mm.then_inc(pv_done, 1)

                    def rest(h, n):
                        if n == 0:
                            turn_probs(h, 2)
                        if n == 1:
                            weighted_values(h, 0)
                            turn_probs(h, 3)
                        if n == 3:
                            weighted_values(h, 1)

                    def head(h, before):
                        for n in range(2 * MEM_C):
                            c = n // 2
                            if isinstance(h, int) and n == 0:
                                pe.wait_ge(ml_done, KC)
                            a, b, width = (m_hi, m_lo, NMEM) if c in (K, V) else (hi, lo, SEQ)
                            unit(pe, C0 + MEM_C * h + c, (C0 + c) % 2, n % 2, a, b, width=width)
                            if before is not None:
                                rest(before, n)
                            if n == 4:
                                turn_values(h)
                            if n == 5:
                                scores(h, 0)
                                scores(h, 1)
                            if n == 6:
                                turn_probs(h, 0)
                                scores(h, 2)
                            if n == 7:
                                turn_probs(h, 1)
                                scores(h, 3)
                    head(0, None)
                    with pe.Fori(1, MEM_HEADS) as h:
                        head(h, h - 1)
                    for n in range(4):
                        rest(MEM_HEADS - 1, n)

                @block.scalar
                def _(act):
                    def exps(h, p_):
                        N = NP * h + p_
                        b = p_ % 2
                        act.wait_ge(neg_done, N + 1)
                        need(act, tr_done, N - 1)
                        for t in range(2):
                            act.activation(p[b][:, t, :], s_ps[:, b * 512 + t * NMEM:b * 512 + (t + 1) * NMEM], ACT.Exp,
                                           bias=nm[:, b, t:t + 1], scale=SCALE, accum_out=l[:, b, t:t + 1])\
                                .then_inc(exp_done, 1)

                    def move_probs(h, p_):
                        N = NP * h + p_
                        s, b = p_ // 2, p_ % 2
                        act.wait_ge(tr_done, N + 1)
                        if p_ == 0:
                            need(act, pv_done, NS * h)
                        act.activation(pT[s][:, :, b * 256:(b + 1) * 256],
                                       t_ps[:, b * 512:(b + 1) * 512].rearrange("p (m q) -> p m q", q=256),
                                       ACT.Copy).then_inc(pt_ready, 1)

                    def move(h, n):
                        c, s = n // 2, n % 2
                        j = C0 + MEM_C * h + c
                        if c == G:
                            if s == 1:
                                act.wait_ge(z_free[0], j + 1)
                            gate_exp(act, s, j, eg, ge_done)
                            return
                        act.wait_ge(z_ready[s], j + 1)
                        if n == 0:
                            need(act, qk_done, NP * h)
                        if c == V:
                            need(act, vtr_done, h)
                        if c == Q:
                            out, src = q[:, s * SEQ:(s + 1) * SEQ], z_ps[s][:]
                        else:
                            out, src = (kT if c == K else vT)[:, s * NMEM:(s + 1) * NMEM], z_ps[s][:, 0:NMEM]
                        act.activation(out, src, ACT.Copy).then_inc(z_free[s], 1)

                    def rest(h, n):
                        if n == 0:
                            exps(h, 2)
                            move_probs(h, 1)
                            exps(h, 3)
                        if n == 1:
                            move_probs(h, 2)
                        if n == 2:
                            move_probs(h, 3)

                    def head(h, before, last):
                        for n in range(2 * MEM_C):
                            c = n // 2
                            if n % 2 == 0:
                                ahead = C0 + MEM_C * h + c + 1
                                split_hi(act, ahead, halves(C0, MEM_C, h, c + 1), (C0 + c + 1) % 2,
                                         nk=FC if last and c == MEM_C - 1 else KC)
                            if before is not None:
                                rest(before, n)
                            if n == 6:
                                exps(h, 0)
                                exps(h, 1)
                            if n == 7:
                                move_probs(h, 0)
                            move(h, n)
                    act.wait_ge(mh_in, 16)
                    for k in range(KC):
                        act.wait_ge(mg_done, k + 1)
                        act.activation(m_hi[:, k, :], m_g[k % 2][:], ACT.Copy).then_inc(mh_done, 1)
                    act.preload_act_table(ACT.Exp)
                    head(0, None, False)
                    with act.Fori(1, MEM_HEADS - 1) as h:
                        head(h, h - 1, False)
                    head(MEM_HEADS - 1, MEM_HEADS - 2, True)
                    for n in range(3):
                        rest(MEM_HEADS - 1, n)

                @block.vector
                def _(dve):
                    def softmax_in(h, p_):
                        N = NP * h + p_
                        b = p_ % 2
                        dve.wait_ge(qk_done, N + 1)
                        dve.tensor_reduce(mx[:, b, :], s_ps[:, b * 512:(b + 1) * 512].rearrange("p (t m) -> p t m", t=2),
                                          AX, ALU.max).then_inc(max_done, 1)
                        dve.wait_ge(max_done, N + 1)
                        dve.tensor_scalar(nm[:, b, :], mx[:, b, :], -SCALE, None, ALU.mult).then_inc(neg_done, 1)

                    def softmax_out(h, p_):
                        N = NP * h + p_
                        b = p_ % 2
                        dve.wait_ge(exp_done, 2 * N + 2)
                        dve.reciprocal(rl[:, b, :], l[:, b, :]).then_inc(rl_done, 1)
                        dve.wait_ge(rl_done, N + 1)
                        for t in range(2):
                            dve.tensor_scalar(p[b][:, t, :], p[b][:, t, :], rl[:, b, t:t + 1], None, ALU.mult)\
                                .then_inc(p_ready, 1)

                    def finish(h, s):
                        dve.wait_ge(pv_done, NS * h + s + 1)
                        tok = slice(s * SEQ, (s + 1) * SEQ)
                        out, o, g = y[:, tok], o_ps[:], gate[:, tok]
                        if i == 0:
                            out = out.rearrange("p (i r) -> p r i", r=RES)
                            o, g = (a.rearrange("p (r i) -> p r i", r=RES) for a in (o, g))
                        dve.tensor_tensor(out, o, g, ALU.mult).then_inc(y_done, 1)

                    def rest(h, n):
                        if n == 0:
                            softmax_in(h, 2)
                            softmax_out(h, 2)
                            softmax_in(h, 3)
                            softmax_out(h, 3)
                        if n == 2:
                            finish(h, 0)
                        if n == 4:
                            finish(h, 1)

                    def head(h, before, last):
                        for n in range(2 * MEM_C):
                            c = n // 2
                            if n % 2 == 0:
                                split_lo(dve, C0 + MEM_C * h + c + 1, (C0 + c + 1) % 2,
                                         nk=FC if last and c == MEM_C - 1 else KC)
                            if before is not None:
                                rest(before, n)
                            if n == 5:
                                dve.wait_ge(vtr_done, h + 1)
                                need(dve, pv_done, NS * h)
                                dve.tensor_copy(v[:], v_ps[:].rearrange("p (t e) -> p t e", e=HD)).then_inc(v_ready, 1)
                            if n == 6:
                                for p_ in (0, 1):
                                    softmax_in(h, p_)
                                for p_ in (0, 1):
                                    softmax_out(h, p_)
                            if c == G:
                                s = n % 2
                                if s == 0:
                                    need(dve, y_done, NS * h)
                                    need(dve, y_stored, 16 * h)
                                gate_silu(dve, s, gate[:, s * SEQ:(s + 1) * SEQ], NS * h + s, eg, ge_done, gstep)
                    dve.wait_ge(mh_in, 16)
                    for k in range(KC):
                        need(dve, ml_done, k - 1)
                        dve.tensor_scalar(m_g[k % 2][:], m_hat[:, k, :], gains[:, 2 * i + 1, k:k + 1], None, ALU.mult)\
                            .then_inc(mg_done, 1)
                        dve.wait_ge(mh_done, k + 1)
                        dve.tensor_tensor(m_lo[:, k, :], m_g[k % 2][:], m_hi[:, k, :].bitcast(F32), ALU.subtract)\
                            .then_inc(ml_done, 1)
                    head(0, None, False)
                    with dve.Fori(1, MEM_HEADS - 1) as h:
                        head(h, h - 1, False)
                    head(MEM_HEADS - 1, MEM_HEADS - 2, True)
                    for n in range(5):
                        rest(MEM_HEADS - 1, n)

        def output_projection(i, xT, st):
            tag = "ab"[i]
            y_hi = sb(tag + "y_hi", [P, FC, TOK], F32R, stack=st)
            y_lo = sb(tag + "y_lo", [P, FC, TOK], F32R, stack=st)
            y_raw = [sb(f"{tag}y_raw{b}", [P, TOK], stack=st) for b in range(2)]
            res = sb(tag + "res", [P, 2, TOK], stack=st)
            y_in = [sem(f"{tag}y_in{b}") for b in range(2)]
            yh, yl, res_in, x_stored = (sem(f"{tag}out_" + n) for n in ("yh", "yl", "res_in", "x_stored"))
            res_in2 = sem(f"{tag}out_res_in2")
            w = A[tag + "_wout"][0]
            C0 = C_OUT[i]
            last_stage = i == 1
            PAIRS = KC // 2
            block = st.enter_context(nc.Block())
            rin = (res_in, res_in2)

            @block.sync
            def _(sp):
                for f in range(FC):
                    need(sp, yl, f - 1)
                    sp.dma_start(y_raw[f % 2][:], y_scratch[i][f]).then_inc(y_in[f % 2], 16)

                def pair(d2, start=0):
                    for b in range(start, 2):
                        w_load(sp, w, (2 * d2 + b) * P, (C0 + b) % 2, C0 + 2 * d2 + b, nk=FC)
                pair(0, start=1)
                with sp.Fori(1, PAIRS) as d2:
                    pair(d2)
                if not last_stage:
                    w_load(sp, A["b_win"][0], GLR, C_LR % 2, C_LR)

            @block.gpsimd
            def _(pool):
                def load(c, b):
                    if not isinstance(c, int) or c >= 2:
                        for s in range(NS):
                            pool.wait_ge(z_free[s], C0 + c - 1)
                    pool.dma_start(res[:, b, :], xt_scratch[:, c, :]).then_inc(rin[b], 16)
                load(0, 0)
                load(1, 1)
                with pool.Fori(1, PAIRS) as d2:
                    for b in range(2):
                        load(2 * d2 + b, b)
                if not last_stage:
                    for s in range(NS):
                        pool.wait_ge(z_free[s], C0 + KC)
                    pool.dma_start(xt_scratch, xT[:]).then_inc(x_stored, 16)
                    pool.wait_ge(x_stored, 16)

            @block.tensor
            def _(pe):
                def pair(d2):
                    for n in range(4):
                        unit(pe, C0 + 2 * d2 + n // 2, (C0 + n // 2) % 2, n % 2, y_hi, y_lo, nk=FC)
                pe.wait_ge(yl, FC)
                pair(0)
                with pe.Fori(1, PAIRS) as d2:
                    pair(d2)

            @block.scalar
            def _(act):
                for f in range(FC):
                    act.wait_ge(y_in[f % 2], 16 * (f // 2) + 16)
                    act.activation(y_hi[:, f, :], y_raw[f % 2][:], ACT.Copy).then_inc(yh, 1)

                def pair(d2, end):
                    for b in range(2):
                        if not (end and b == 1):
                            split_hi(act, C0 + 2 * d2 + b + 1, halves(C0, 2, d2, b + 1), (C0 + b + 1) % 2, nk=FC)
                pair(0, False)
                with act.Fori(1, PAIRS - 1) as d2:
                    pair(d2, False)
                pair(PAIRS - 1, True)

            @block.vector
            def _(dve):
                for f in range(FC):
                    dve.wait_ge(yh, f + 1)
                    dve.tensor_tensor(y_lo[:, f, :], y_raw[f % 2][:], y_hi[:, f, :].bitcast(F32), ALU.subtract)\
                        .then_inc(yl, 1)

                def pair(d2, end):
                    for n in range(4):
                        b, s = n // 2, n % 2
                        if s == 0 and not (end and b == 1):
                            split_lo(dve, C0 + 2 * d2 + b + 1, (C0 + b + 1) % 2, nk=FC)
                        dve.wait_ge(rin[b], 16 * d2 + 16)
                        dve.wait_ge(z_ready[s], C0 + 2 * d2 + b + 1)
                        dve.tensor_tensor(xT[:, 2 * d2 + b, s * SEQ:(s + 1) * SEQ], z_ps[s][:],
                                          res[:, b, s * SEQ:(s + 1) * SEQ], ALU.add).then_inc(z_free[s], 1)
                pair(0, False)
                with dve.Fori(1, PAIRS - 1) as d2:
                    pair(d2, False)
                pair(PAIRS - 1, True)

        gla = make_gla(nc, A, locals())

        load_and_transpose()
        with ExitStack() as layer:
            hi = sb("ah_hi", [P, KC, TOK], F32R, stack=layer)
            lo = sb("ah_lo", [P, KC, TOK], F32R, stack=layer)
            with ExitStack() as st:
                xa = sb("xa", [P, KC, TOK], stack=st)
                norm_split("an", xa, 0, hi, lo, True, C_DIL, st, load_x=True)
            dilated(hi, lo)
            memory(0, hi, lo)
        with ExitStack() as layer:
            xb = sb("xb", [P, KC, TOK], stack=layer)
            with ExitStack() as st:
                output_projection(0, xb, st)
            with ExitStack() as st:
                pass
        with ExitStack() as layer:
            hi = sb("bh_hi", [P, KC, TOK], F32R, stack=layer)
            lo = sb("bh_lo", [P, KC, TOK], F32R, stack=layer)
            with ExitStack() as st:
                xa = sb("xb2", [P, KC, TOK], stack=st)
                norm_split("bn", xa, 2, hi, lo, False, C_LR, st, load_x=True)
            gla(hi, lo)
            memory(1, hi, lo)
        with ExitStack() as layer:
            xb = sb("xc", [P, KC, TOK], stack=layer)
            with ExitStack() as st:
                output_projection(1, xb, st)
            final_norm(nc, A, xb, sb, sem, ident, ones, gains, eps_col, s_ps, t_ps, o_ps, v_ps)


def final_norm(nc, A, xT, sb, sem, ident, ones, gains, eps_col, s_ps, t_ps, o_ps, v_ps):
    with ExitStack() as st:
        sq = [sb(f"f_sq{i}", [P, SEQ], stack=st) for i in range(2)]
        rstd = sb("f_rstd", [P, TOK], stack=st)
        rows = [sb(f"f_rows{i}", [P, D], stack=st) for i in range(2)]
        (sq_done, sum_done, sd_done, r_done, n_done, turned, moved) = (
            sem("f_" + n) for n in ("sq_done", "sum_done", "sd_done", "r_done", "n_done", "turned", "moved"))
        stored = [sem("f_stored0"), sem("f_stored1")]
        block = st.enter_context(nc.Block())
        banks = (o_ps, v_ps)
        turn_ps = (s_ps, t_ps)

        @block.scalar
        def _(act):
            for n in range(NS * KC):
                s, k = n // KC, n % KC
                need(act, sum_done, n - 1)
                act.activation(sq[n % 2][:], xT[:, k, s * SEQ:(s + 1) * SEQ], ACT.Square).then_inc(sq_done, 1)
            for s in range(NS):
                act.wait_ge(sum_done, KC * s + KC)
                act.activation(rstd[:, s * SEQ:(s + 1) * SEQ], banks[s][:], ACT.Sqrt, bias=eps_col[:],
                               scale=1.0 / D).then_inc(sd_done, 1)
            for t in range(NT):
                act.wait_ge(turned, t + 1)
                need(act, stored[t % 2], 16 * (t // 2))
                act.activation(rows[t % 2][:], turn_ps[t % 2][:], ACT.Copy).then_inc(moved, 1)

        @block.tensor
        def _(pe):
            for n in range(NS * KC):
                pe.wait_ge(sq_done, n + 1)
                pe.matmul(banks[n // KC][:], ones[:], sq[n % 2][:], start=(n % KC == 0),
                          stop=(n % KC == KC - 1)).then_inc(sum_done, 1)
            for t in range(NT):
                need(pe, moved, t - 1)
                pe.wait_ge(n_done, KC * (t // (SEQ // P) + 1))
                for k in range(KC):
                    tr = pe.transpose(turn_ps[t % 2][:, k * P:(k + 1) * P], xT[:, k, t * P:(t + 1) * P], ident[:])
                tr.then_inc(turned, 1)

        @block.vector
        def _(dve):
            for s in range(NS):
                tok = slice(s * SEQ, (s + 1) * SEQ)
                dve.wait_ge(sd_done, s + 1)
                dve.reciprocal(rstd[:, tok], rstd[:, tok]).then_inc(r_done, 1)
                dve.wait_ge(r_done, s + 1)
                dve.wait_ge(sum_done, NS * KC)
                for k in range(KC):
                    dve.scalar_tensor_tensor(out=xT[:, k, tok], in0=xT[:, k, tok], scalar=gains[:, 4, k:k + 1],
                                             in1=rstd[:, tok], op0=ALU.mult, op1=ALU.mult).then_inc(n_done, 1)

        @block.sync
        def _(sp):
            for t in range(NT):
                out = A["y_prompt" if t < SEQ // P else "y_sample"][0]
                i = t % (SEQ // P)
                sp.wait_ge(moved, t + 1)
                sp.dma_start(out[i * P:(i + 1) * P, :], rows[t % 2][:]).then_inc(stored[t % 2], 16)
            for b in range(2):
                sp.wait_ge(stored[b], 16 * (NT // 2))


def make_gla(nc, A, env):
    sb, sem, unit, w_load = env["sb"], env["sem"], env["unit"], env["w_load"]
    split_hi, split_lo, gate_exp, gate_silu = env["split_hi"], env["split_lo"], env["gate_exp"], env["gate_silu"]
    z_ps, s_ps, t_ps, o_ps, v_ps = env["z_ps"], env["s_ps"], env["t_ps"], env["o_ps"], env["v_ps"]
    z_ready, z_free, ident, ones = env["z_ready"], env["z_free"], env["ident"], env["ones"]
    carrier = env["carrier"]
    w_raw, onorm, eps_col, y_scratch = env["w_raw"], env["onorm"], env["eps_col"], env["y_scratch"]

    NL = len(LEVELS)
    NE = NL + 1
    NLD = NL + 2
    TPS = SEQ // P
    QS = float(GDK) ** -0.5
    Q, K, V, G = 0, 1, 2, 4
    SLOTS = 2 * GLA_C
    FW, BW = 0, 1
    ST = TPS - 1

    def stage(hi, lo):
        with ExitStack() as st:
            def buf(name, shape):
                return sb("g_" + name, shape, stack=st)

            q, k = buf("q", [P, TOK]), buf("k", [P, TOK])
            vT = buf("vT", [P, TOK])
            v = buf("v", [P, NT, GDV])
            gate = buf("gate", [P, 2, TOK])
            eg = buf("eg", [P, SEQ])
            b = [buf("b_f", [P, TOK]), buf("b_b", [P, TOK])]
            E = [buf("E0", [P, 2, TOK]), buf("E1", [P, 2, TOK])]
            att = buf("att", [P, NT, P])
            masks = sb("g_masks", [P, NL + 1, P], U32, stack=st)
            qi = buf("qi", [P, 2, TOK])
            kd = buf("kd", [P, 2, NT, P])
            out_sb = kd[:].rearrange("p s t e -> p s (t e)").rearrange("p s (f i) -> p s f i", f=2)
            S = buf("S", [P, 2, NS, ST, GDV])
            rstd = buf("rstd", [P, SEQ])
            lrT = sb("g_lrT", [2 * RANK, TOK], stack=st)
            wg = sb("g_wg", [2 * RANK, 2, GDK], stack=st)
            bg, bgh = buf("bg", [P, 2, GLA_HEADS]), buf("bgh", [P, 2])
            starts = buf("starts", [P, SEQ])
            dcol, dec = buf("dcol", [P, 2, NT]), buf("dec", [P, 2, NT])
            sq = [w_raw[i][:, KC:FC, :].rearrange("p k c -> p (k c)") for i in range(2)]

            e0 = E[0][:].rearrange("p a t -> p (a t)")
            e1 = E[1][:].rearrange("p a t -> p (a t)")
            SH = 4
            g = [e0[:, 0:TOK], e1[:, SH:SH + TOK]]
            L = [e0[:, TOK + s * SEQ:TOK + (s + 1) * SEQ] for s in range(NS)]

            (bgh_done, bg_in, c_in, wg_zero, wg_in, x_done, min_done, abs_done, ex_done, ln_done, g_done, scan_done, dcol_done,
             dec_done, sub_done, e_done, op_done, qsub_done, qe_done, qi_done, zero_done, lev_done, mask_done, kd_ready,
             st_mm, st_done, vtr_done, v_ready, out_done, out_moved, sq_done, ssq_done, sd_done, r_done, t_done, y_done,
             y_stored, ge_done, gstep) = (sem("gla_" + n) for n in (
                 "bgh_done", "bg_in", "c_in", "wg_zero", "wg_in", "x_done", "min_done", "abs_done", "ex_done", "ln_done",
                 "g_done", "scan_done", "dcol_done", "dec_done", "sub_done", "e_done", "op_done", "qsub_done",
                 "qe_done", "qi_done", "zero_done", "lev_done", "mask_done", "kd_ready", "st_mm", "st_done",
                 "vtr_done", "v_ready", "out_done", "out_moved", "sq_done", "ssq_done", "sd_done", "r_done",
                 "t_done", "y_done", "y_stored", "ge_done", "gstep"))
            w = A["b_win"][0]
            block = st.enter_context(nc.Block())

            def toks(s):
                return slice(s * SEQ, (s + 1) * SEQ)

            def chunk(h, c):
                return C_GLA + GLA_C * h + c

            def slot_of(c):
                return (C_GLA + c) % 2

            @block.sync
            def _(sp):
                sp.dma_start(masks[:], A["c_masks"]).then_inc(c_in, 16)
                sp.dma_start(starts[:], A["c_starts"][:, 0:SEQ]).then_inc(c_in, 16)

                def head(h):
                    cols = [GQ + h * GDK, GK + h * GDK, GV + h * GDV, GV + h * GDV + P, GATE_B + h * GDV,
                            GATE_B + h * GDV + P]
                    for c in range(GLA_C):
                        w_load(sp, w, cols[c], slot_of(c), chunk(h, c))
                head(0)
                with sp.Fori(1, GLA_HEADS) as h:
                    head(h)
                w_load(sp, A["b_wmem"][0], 0, C_MEM[1] % 2, C_MEM[1])

            @block.gpsimd
            def _(pool):
                pool.memset(wg[:], 0.0).then_inc(wg_zero, 1)
                for d, n in enumerate(("b_bg_f", "b_bg_b")):
                    pool.dma_start(bg[:, d, :], A[n][0].rearrange("(h p) -> p h", p=P)).then_inc(bg_in, 16)
                pool.wait_ge(wg_zero, 1)

                def load_gates(col):
                    for d, n in enumerate(("b_wg_f", "b_wg_b")):
                        pool.dma_start(wg[d * RANK:(d + 1) * RANK, d, :], A[n][0][:, bass.ds(col, GDK)])\
                            .then_inc(wg_in, 16)

                def operands(h, n):
                    pool.wait_ge(e_done, NE * h + n + 1)
                    if n == 0:
                        for s in range(NS):
                            pool.wait_ge(z_free[s], chunk(h, K) + 1)
                    a = q if n < NL else k
                    pool.tensor_tensor(E[n % 2][:, 0, :], E[n % 2][:, 0, :], a[:], ALU.mult)
                    pool.tensor_tensor(E[n % 2][:, 1, :], E[n % 2][:, 1, :], k[:], ALU.mult).then_inc(op_done, 1)

                def query_decays(h):
                    pool.wait_ge(qe_done, h + 1)
                    pool.tensor_tensor(qi[:, 0, :], qi[:, 0, :], q[:], ALU.mult)
                    pool.tensor_tensor(qi[:, 1, :], qi[:, 1, :], q[:], ALU.mult).then_inc(qi_done, 1)

                def squares(h, s):
                    pool.wait_ge(out_moved, 4 * h + 2 * s + 2)
                    if s == 1:
                        pool.wait_ge(ssq_done, 2 * h + 1)
                    for f in range(2):
                        pool.tensor_tensor(sq[f], out_sb[:, s, f, :], out_sb[:, s, f, :], ALU.mult).then_inc(sq_done, 1)

                def rest(h, n):
                    if n == 4:
                        squares(h, 0)
                    if n == 5:
                        squares(h, 1)
                    if n == 7:
                        pool.wait_ge(y_done, 4 * h + 4)
                        for f in range(2):
                            pool.dma_start(y_scratch[1][2 * h + f], gate[:, f, :]).then_inc(y_stored, 16)

                def head(h, before, col_next):
                    for n in range(SLOTS):
                        if before is not None:
                            rest(before, n)
                        if n == 4:
                            pool.wait_ge(x_done, 2 * h + 2)
                            load_gates(col_next)
                        if 4 <= n < 4 + NE:
                            operands(h, n - 4)
                        if n == 9:
                            query_decays(h)
                            need(pool, ssq_done, 2 * h)

                load_gates(0)
                head(0, None, GDK)
                with pool.Fori(1, GLA_HEADS - 1) as h:
                    head(h, h - 1, (h + 1) * GDK)
                head(GLA_HEADS - 1, GLA_HEADS - 2, 0)
                for n in range(8):
                    rest(GLA_HEADS - 1, n)
                pool.wait_ge(y_stored, 32 * GLA_HEADS)
                pool.wait_ge(wg_in, 32 * (GLA_HEADS + 1))

            @block.tensor
            def _(pe):
                def gates(h):
                    pe.wait_ge(wg_in, 32 * h + 32)
                    need(pe, kd_ready, 2 * h)
                    for d, dst in enumerate((s_ps, t_ps)):
                        for s in range(NS):
                            mm = pe.matmul(dst[:, toks(s)], wg[:, d, :], lrT[:, toks(s)], start=True, stop=True)
                        mm.then_inc(x_done, 1)

                def level(h, i):
                    dst = (s_ps, t_ps)[i % 2]
                    if i == 0:
                        for s in range(NS):
                            pe.wait_ge(z_free[s], chunk(h, K) + 1)
                        a, c = k, q
                    else:
                        pe.wait_ge(op_done, NE * h + i)
                        a, c = E[(i - 1) % 2][:, 1, :], E[(i - 1) % 2][:, 0, :]
                    if i < 2:
                        pe.wait_ge(abs_done, 4 * h + 2 * i + 2)
                    else:
                        pe.wait_ge(mask_done, (NL + 1) * h + i - 1)
                    for t in range(NT):
                        tok = slice(t * P, (t + 1) * P)
                        mm = pe.matmul(dst[:, tok], a[:, tok], c[:, tok], start=True, stop=True)
                    mm.then_inc(lev_done, 1)

                def turn_keys(h):
                    pe.wait_ge(op_done, NE * h + NE)
                    pe.wait_ge(mask_done, (NL + 1) * (h + 1))
                    for d, dst in enumerate((s_ps, t_ps)):
                        for t in range(NT):
                            tr = pe.transpose(dst[:, t * P:(t + 1) * P], E[NL % 2][:, d, t * P:(t + 1) * P], ident[:])
                    tr.then_inc(lev_done, 1)

                def turn_values(h, m):
                    f, s = m // 2, m % 2
                    pe.wait_ge(z_free[s], chunk(h, V + f) + 1)
                    need(pe, v_ready, 4 * h + m)
                    if m == 0:
                        need(pe, out_moved, 4 * h)
                    for i in range(TPS):
                        t = s * TPS + i
                        tr = pe.transpose(v_ps[:, i * P:(i + 1) * P], vT[:, t * P:(t + 1) * P], ident[:])
                    tr.then_inc(vtr_done, 1)

                def states(h, r):
                    s, i = r // ST, r % ST
                    dst = (o_ps, v_ps)[r % 2]
                    if r == 0:
                        pe.wait_ge(kd_ready, 2 * h + 2)
                        pe.wait_ge(v_ready, 4 * h + 4)
                    if r >= 2:
                        pe.wait_ge(st_done, 2 * ST * h + r - 1)
                    for d in range(2):
                        t = s * TPS + (i if d == FW else TPS - 1 - i)
                        mm = pe.matmul(dst[:, d * GDV:(d + 1) * GDV], kd[:, d, t, :], v[:, t, :], start=True, stop=True)
                    mm.then_inc(st_mm, 1)

                def outputs(h, s):
                    for f, dst in enumerate((o_ps, v_ps)):
                        if s == 0 and f == 0:
                            pe.wait_ge(st_done, 2 * ST * (h + 1))
                            pe.wait_ge(qi_done, h + 1)
                        if s == 1:
                            pe.wait_ge(out_moved, 4 * h + 2)
                        cols = slice(f * P, (f + 1) * P)
                        for i in range(TPS):
                            t = s * TPS + i
                            tok = slice(t * P, (t + 1) * P)
                            dt = dst[:, i * P:(i + 1) * P]
                            mm = pe.matmul(dt, v[:, t, cols], att[:, t, :], start=(i == 0), stop=False,
                                           skip_group_check=True)
                            if i > 0:
                                mm = pe.matmul(dt, S[:, FW, s, i - 1, cols], qi[:, 0, tok], start=False,
                                               stop=(i == TPS - 1), skip_group_check=True)
                            if i < TPS - 1:
                                mm = pe.matmul(dt, S[:, BW, s, TPS - 2 - i, cols], qi[:, 1, tok], start=False,
                                               stop=False, skip_group_check=True)
                        mm.then_inc(out_done, 1)

                def sum_squares(h, s):
                    pe.wait_ge(sq_done, 4 * h + 2 * s + 2)
                    if s == 0:
                        pe.wait_ge(out_moved, 4 * h + 4)
                    else:
                        pe.wait_ge(sd_done, 2 * h + 1)
                    pe.matmul(o_ps[:], ones[:], sq[0], start=True, stop=False)
                    pe.matmul(o_ps[:], ones[:], sq[1], start=False, stop=True).then_inc(ssq_done, 1)

                def rest(h, n):
                    if n == 0:
                        level(h, NL)
                        turn_keys(h)
                    if n == 2:
                        for r in range(ST):
                            states(h, r)
                    if n == 3:
                        for r in range(ST, 2 * ST):
                            states(h, r)
                        outputs(h, 0)
                    if n == 4:
                        outputs(h, 1)
                    if n in (5, 6):
                        sum_squares(h, n - 5)

                def head(h, before):
                    for n in range(SLOTS):
                        c = n // 2
                        unit(pe, chunk(h, c), slot_of(c), n % 2, hi, lo)
                        if before is not None:
                            rest(before, n)
                        if n == 1:
                            gates(h)
                        if n == 9:
                            need(pe, st_done, 2 * ST * h)
                            need(pe, sd_done, 2 * h)
                        if 5 <= n < 9:
                            turn_values(h, n - 5)
                        if n >= 5:
                            level(h, n - 5)
                for s in range(NS):
                    unit(pe, C_LR, C_LR % 2, s, hi, lo)
                for s in range(NS):
                    pe.wait_ge(z_free[s], C_LR + 1)
                head(0, None)
                with pe.Fori(1, GLA_HEADS) as h:
                    head(h, h - 1)
                for n in range(7):
                    rest(GLA_HEADS - 1, n)

            @block.scalar
            def _(act):
                def log_gates(h, d):
                    src = (s_ps, t_ps)[d]
                    act.wait_ge(min_done, 2 * h + d + 1)
                    for s in range(NS):
                        n = 4 * h + 2 * d + s
                        if d == 1:
                            act.wait_ge(g_done, 4 * h + s + 1)
                        act.activation(L[s], src[:, toks(s)], ACT.Abs, bias=bgh[:, d:d + 1]).then_inc(abs_done, 1)
                        act.wait_ge(abs_done, n + 1)
                        act.activation(L[s], L[s], ACT.Exp, scale=-1.0).then_inc(ex_done, 1)
                        act.wait_ge(ex_done, n + 1)
                        act.activation(L[s], L[s], ACT.Ln, bias=1.0).then_inc(ln_done, 1)

                def decays(h):
                    act.wait_ge(dcol_done, 2 * h + 2)
                    need(act, st_done, 2 * ST * h)
                    act.activation(dec[:], dcol[:], ACT.Exp, scale=1.0 / TAU).then_inc(dec_done, 1)

                def exps(h, n):
                    act.wait_ge(sub_done, NE * h + n + 1)
                    if n < NL:
                        act.activation(E[n % 2][:], E[n % 2][:], ACT.Exp, scale=1.0 / TAU).then_inc(e_done, 1)
                    else:
                        act.activation(E[n % 2][:, 1, :], b[BW][:], ACT.Exp, scale=1.0 / TAU)
                        act.activation(E[n % 2][:, 0, :], E[n % 2][:, 0, :], ACT.Exp, scale=1.0 / TAU).then_inc(e_done, 1)

                def query_exps(h):
                    act.wait_ge(qsub_done, h + 1)
                    act.activation(qi[:, 0, :], b[FW][:], ACT.Exp, scale=1.0 / TAU)
                    act.activation(qi[:, 1, :], qi[:, 1, :], ACT.Exp, scale=1.0 / TAU).then_inc(qe_done, 1)

                def move_keys(h):
                    act.wait_ge(lev_done, NLD * (h + 1))
                    for d, src in enumerate((s_ps, t_ps)):
                        act.activation(kd[:, d, :, :], src[:].rearrange("p (t e) -> p t e", e=P), ACT.Copy)\
                            .then_inc(kd_ready, 1)

                def move_outputs(h, s):
                    for f, src in enumerate((o_ps, v_ps)):
                        act.wait_ge(out_done, 4 * h + 2 * s + f + 1)
                        act.activation(out_sb[:, s, f, :], src[:], ACT.Copy).then_inc(out_moved, 1)

                def root(h, s):
                    act.wait_ge(ssq_done, 2 * h + s + 1)
                    if s == 1:
                        act.wait_ge(t_done, 4 * h + 2)
                    act.activation(rstd[:], o_ps[:], ACT.Sqrt, bias=eps_col[:], scale=1.0 / GDV).then_inc(sd_done, 1)

                def rest(h, n):
                    if n == 0:
                        exps(h, NL)
                    if n == 1:
                        move_keys(h)
                    if n in (4, 5):
                        move_outputs(h, n - 4)
                    if n in (6, 7):
                        root(h, n - 6)

                def move(h, n):
                    c, s = n // 2, n % 2
                    j = chunk(h, c)
                    if c >= G:
                        if n > 2 * G:
                            act.wait_ge(z_free[1 - s], j + s)
                        gate_exp(act, s, j, eg, ge_done)
                        return
                    act.wait_ge(z_ready[s], j + 1)
                    if n == 0:
                        need(act, op_done, NE * h)
                    if c == V or c == V + 1:
                        need(act, vtr_done, 4 * h + 2 * (c - V) + s - 1)
                    if c == Q:
                        act.activation(q[:, toks(s)], z_ps[s][:], ACT.Copy, scale=QS).then_inc(z_free[s], 1)
                    else:
                        act.activation((k if c == K else vT)[:, toks(s)], z_ps[s][:], ACT.Copy).then_inc(z_free[s], 1)

                def head(h, before):
                    for n in range(SLOTS):
                        if n % 2 == 0:
                            split_hi(act, chunk(h, n // 2) + 1, halves(C_GLA, GLA_C, h, n // 2 + 1), slot_of(n // 2 + 1))
                        if before is not None:
                            rest(before, n)
                        if n == 2:
                            log_gates(h, FW)
                            log_gates(h, BW)
                        if n == 4:
                            decays(h)
                        if 4 <= n < 4 + NL:
                            exps(h, n - 4)
                        if n == 9:
                            query_exps(h)
                            need(act, y_done, 4 * h)
                        move(h, n)
                split_hi(act, C_GLA, C_GLA // 2, C_GLA % 2)
                act.wait_ge(bg_in, 16 * 2)
                for s in range(NS):
                    act.wait_ge(z_ready[s], C_LR + 1)
                    act.activation(lrT[:, toks(s)], z_ps[s][0:2 * RANK, :], ACT.Copy).then_inc(z_free[s], 1)
                head(0, None)
                with act.Fori(1, GLA_HEADS) as h:
                    head(h, h - 1)
                for n in range(8):
                    rest(GLA_HEADS - 1, n)

            @block.vector
            def _(dve):
                def minima(h, d):
                    src = (s_ps, t_ps)[d]
                    dve.wait_ge(x_done, 2 * h + d + 1)
                    need(dve, lev_done, NLD * h)
                    dve.tensor_scalar(g[d], src[:], bgh[:, d:d + 1], 0.0, ALU.add, ALU.min).then_inc(min_done, 1)

                def log_sums(h, d):
                    for s in range(NS):
                        n = 4 * h + 2 * d + s
                        dve.wait_ge(ln_done, n + 1)
                        dve.tensor_tensor(g[d][:, toks(s)], g[d][:, toks(s)], L[s], ALU.subtract).then_inc(g_done, 1)
                        dve.wait_ge(g_done, n + 1)
                        if d == FW:
                            dve.tensor_tensor_scan(b[FW][:, toks(s)], starts[:], g[FW][:, toks(s)], 0.0, ALU.mult,
                                                   ALU.add).then_inc(scan_done, 1)
                        else:
                            dve.tensor_tensor_scan(b[BW][:, toks(s)], e1[:, SH - 1 + s * SEQ:SH - 1 + (s + 1) * SEQ],
                                                   starts[:], 0.0, ALU.add, ALU.mult).then_inc(scan_done, 1)

                def tile_sums(h):
                    dve.wait_ge(scan_done, 4 * h + 4)
                    need(dve, dec_done, h)
                    last = [x.rearrange("p (t i) -> p t i", i=P)[:, :, P - 1] for x in (b[FW][:], b[BW][:], g[BW])]
                    dve.tensor_copy(dcol[:, FW, :], last[0]).then_inc(dcol_done, 1)
                    dve.tensor_tensor(dcol[:, BW, :], last[1], last[2], ALU.add).then_inc(dcol_done, 1)

                def exponents(h, n):
                    if n == 0:
                        dve.wait_ge(dcol_done, 2 * h + 2)
                    if n >= 2:
                        dve.wait_ge(lev_done, NLD * h + n)
                    if n == NL:
                        bf = b[FW][:].rearrange("p (t i) -> p t i", i=P)
                        dve.tensor_tensor(E[n % 2][:, 0, :].rearrange("p (t i) -> p t i", i=P),
                                          dcol[:, FW, :].rearrange("p (t o) -> p t o", o=1).to_broadcast([P, NT, P]), bf,
                                          ALU.subtract).then_inc(sub_done, 1)
                        return
                    m = LEVELS[n]
                    nb = TOK // (2 * m)

                    def view(a):
                        return a.rearrange("p (n u m) -> p n u m", u=2, m=m)
                    bf, bb = view(b[FW][:]), view(b[BW][:])
                    eq, ek = view(E[n % 2][:, 0, :]), view(E[n % 2][:, 1, :])
                    mid_f = bf[:, :, 0, m - 1:m].to_broadcast([P, nb, m])
                    mid_b = bb[:, :, 1, 0:1].to_broadcast([P, nb, m])
                    dve.tensor_tensor(eq[:, :, 1, :], bf[:, :, 1, :], mid_f, ALU.subtract)
                    dve.tensor_tensor(eq[:, :, 0, :], mid_b, bb[:, :, 0, :], ALU.subtract)
                    dve.tensor_tensor(ek[:, :, 0, :], mid_f, bf[:, :, 0, :], ALU.subtract)
                    dve.tensor_tensor(ek[:, :, 1, :], bb[:, :, 1, :], mid_b, ALU.subtract).then_inc(sub_done, 1)

                def query_exponents(h):
                    need(dve, out_done, 4 * h)
                    dve.tensor_tensor(qi[:, 1, :].rearrange("p (t i) -> p t i", i=P),
                                      dcol[:, BW, :].rearrange("p (t o) -> p t o", o=1).to_broadcast([P, NT, P]),
                                      b[BW][:].rearrange("p (t i) -> p t i", i=P), ALU.subtract).then_inc(qsub_done, 1)

                def pick(h, i):
                    dve.wait_ge(lev_done, NLD * h + i + 1)
                    if i == 0:
                        need(dve, out_done, 4 * h)
                        dve.memset(att[:], 0.0).then_inc(zero_done, 1)
                        dve.wait_ge(zero_done, h + 1)
                    mi = NL if i == 0 else i - 1
                    n = (NL + 1) * h + i
                    need(dve, mask_done, n)
                    carrier(dve)
                    dve.copy_predicated(att[:], masks[:, mi:mi + 1, :].to_broadcast([P, NT, P]),
                                        (s_ps, t_ps)[i % 2][:].rearrange("p (t i) -> p t i", i=P)).then_inc(mask_done, 1)

                def move_values(h, m):
                    f, s = m // 2, m % 2
                    dve.wait_ge(vtr_done, 4 * h + m + 1)
                    if m == 0:
                        need(dve, out_done, 4 * h)
                    dve.tensor_copy(v[:, s * TPS:(s + 1) * TPS, f * P:(f + 1) * P],
                                    v_ps[:].rearrange("p (t e) -> p t e", e=P)).then_inc(v_ready, 1)

                def carry(h, r):
                    s, i = r // ST, r % ST
                    src = (o_ps, v_ps)[r % 2]
                    dve.wait_ge(st_mm, 2 * ST * h + r + 1)
                    if r == 0:
                        dve.wait_ge(dec_done, h + 1)
                    if r > 0:
                        dve.wait_ge(st_done, 2 * ST * h + r)
                    for d in range(2):
                        add = src[:, d * GDV:(d + 1) * GDV]
                        t = s * TPS + (i if d == FW else TPS - 1 - i)
                        if i == 0:
                            ins = dve.tensor_copy(S[:, d, s, 0, :], add)
                        else:
                            ins = dve.scalar_tensor_tensor(out=S[:, d, s, i, :], in0=S[:, d, s, i - 1, :],
                                                           scalar=dec[:, d, t:t + 1], in1=add, op0=ALU.mult, op1=ALU.add)
                    ins.then_inc(st_done, 1)

                def finish(h, s):
                    dve.wait_ge(sd_done, 2 * h + s + 1)
                    dve.reciprocal(rstd[:], rstd[:]).then_inc(r_done, 1)
                    dve.wait_ge(r_done, 2 * h + s + 1)
                    for f in range(2):
                        dve.scalar_tensor_tensor(out=out_sb[:, s, f, :], in0=out_sb[:, s, f, :], scalar=onorm[:, f:f + 1],
                                                 in1=rstd[:], op0=ALU.mult, op1=ALU.mult).then_inc(t_done, 1)
                    for f in range(2):
                        dve.wait_ge(t_done, 4 * h + 2 * s + f + 1)
                        dve.tensor_tensor(gate[:, f, toks(s)], gate[:, f, toks(s)], out_sb[:, s, f, :], ALU.mult)\
                            .then_inc(y_done, 1)

                def rest(h, n):
                    if n == 0:
                        pick(h, NL - 1)
                        pick(h, NL)
                    if n == 3:
                        for r in range(ST):
                            carry(h, r)
                    if n == 4:
                        for r in range(ST, 2 * ST):
                            carry(h, r)
                    if n in (6, 7):
                        finish(h, n - 6)

                def head(h, before):
                    for n in range(SLOTS):
                        if n % 2 == 0:
                            split_lo(dve, chunk(h, n // 2) + 1, slot_of(n // 2 + 1))
                        if before is not None:
                            if n == 0:
                                exponents(before, NL)
                            rest(before, n)
                        if n == 2:
                            need(dve, abs_done, 4 * h)
                            dve.tensor_copy(bgh[:], bg[:, :, bass.ds(h, 1)].rearrange("p d o -> p (d o)")).then_inc(bgh_done, 1)
                            dve.wait_ge(bgh_done, h + 1)
                            minima(h, FW)
                            minima(h, BW)
                            log_sums(h, FW)
                            log_sums(h, BW)
                            tile_sums(h)
                        if 6 <= n < 10:
                            move_values(h, n - 6)
                        if n >= 6:
                            pick(h, n - 6)
                        if n == 9:
                            query_exponents(h)
                        if 4 <= n < 4 + NL:
                            exponents(h, n - 4)
                        if n // 2 >= G:
                            f, s = n // 2 - G, n % 2
                            if n == 2 * G:
                                need(dve, y_stored, 32 * h)
                            gate_silu(dve, s, gate[:, f, toks(s)], 4 * h + 2 * f + s, eg, ge_done, gstep)
                dve.wait_ge(c_in, 16 * 2)
                dve.wait_ge(bg_in, 16 * 2)
                dve.memset(e1[:, SH - 1:SH], 0.0)
                split_lo(dve, C_GLA, C_GLA % 2)
                head(0, None)
                with dve.Fori(1, GLA_HEADS) as h:
                    head(h, h - 1)
                exponents(GLA_HEADS - 1, NL)
                for n in range(8):
                    rest(GLA_HEADS - 1, n)
    return stage


_INS = ["x_prompt", "x_sample", "mem_prompt", "mem_sample", "a_ln", "a_win", "a_mln", "a_wmem", "a_wout", "b_ln",
        "b_win", "b_wg_f", "b_bg_f", "b_wg_b", "b_bg_b", "b_onorm", "b_mln", "b_wmem", "b_wout", "lnf"]
_OUTS = ["y_prompt", "y_sample"]


def constants():
    i = np.arange(P)[:, None]
    j = np.arange(P)[None, :]
    bias = np.empty((P, RES, KEYS), np.float32)
    slope = 0.5 / SCALE
    hidden = -1e30 / SCALE
    for r in range(RES):
        for kt in range(RES):
            d = np.abs((RES * i + r) - (RES * j + kt))
            bias[:, r, kt * P:(kt + 1) * P] = np.where(d <= 64, -d * slope, hidden)
        d = np.abs(i - j)
        bias[:, r, SEQ:SEQ + P] = np.where(d <= 64, -d * slope, hidden)
        bias[:, r, SEQ + P:] = np.where(d % 4 == 0, -(d // 4) * slope, hidden)
    masks = np.zeros((P, len(LEVELS) + 1, P), np.uint32)
    for n, m in enumerate(LEVELS):
        masks[:, n, :] = ((i // (2 * m)) == (j // (2 * m))) & ((i // m) != (j // m))
    masks[:, len(LEVELS), :] = i == j
    starts = np.ones((P, TOK), np.float32)
    starts[:, ::P] = 0.0
    return {"c_ident": np.eye(P, dtype=np.float32), "c_bias": bias, "c_masks": masks, "c_starts": starts}


def kernel(**inputs):
    import concourse.bacc as _bacc
    from concourse.bass_utils import run_bass_kernel_spmd as _run

    nc = _bacc.Bacc("TRN2", target_bir_lowering=False, num_devices=1)
    arrays, args = {}, {}
    given = {n: np.ascontiguousarray(inputs[n]) for n in _INS}
    given.update(constants())
    for name, a in given.items():
        arrays[f"in_{name}"] = a
        args[name] = nc.dram_tensor(f"in_{name}", a.shape, mybir.dt.from_np(a.dtype), kind="ExternalInput").ap()
    for name in _OUTS:
        args[name] = nc.dram_tensor(f"out_{name}", (1, SEQ, D), F32, kind="ExternalOutput").ap()
    build(nc, args)
    r = _run(nc, [arrays], core_ids=[0])
    return tuple(r.results[0][f"out_{name}"] for name in _OUTS)
```

```python
from contextlib import ExitStack

import numpy as np

import concourse.bass as bass
from concourse import mybir

F32 = mybir.dt.float32
F32R = mybir.dt.float32r
U32 = mybir.dt.uint32
ALU = mybir.AluOpType
ACT = mybir.ActivationFunctionType
AX = mybir.AxisListType.X

P = 128
D = 1024
KC = D // P
SEQ = 512
NS = 2
TOK = NS * SEQ
NT = TOK // P
HD = 128
NMEM = 256
MT = NS * NMEM
DIL_HEADS = 8
DIL_W = DIL_HEADS * HD
NG = 3
MEM_HEADS = 4
MEM_W = MEM_HEADS * HD
RES = 4
QKV_A = 3 * NG * DIL_W
GATE_A = QKV_A + MEM_W
BRANCH = 1536
FC = BRANCH // P
GLA_HEADS = 4
GDV = 256
GDK = 128
RANK = 16
GQ, GK, GV = 0, GLA_HEADS * GDK, 2 * GLA_HEADS * GDK
GLR = GV + GLA_HEADS * GDV
GQM = GLR + 2 * RANK
GATE_B = GQM + MEM_W
TAU = 16.0
EPS = 1e-6
SCALE = float(HD) ** -0.5
KEYS = SEQ + 2 * P
LEVELS = [64, 32, 16, 8, 4, 2, 1]

DIL_C, MEM_C, GLA_C = 10, 4, 6
C_DIL = 0
C_MEM = [C_DIL + DIL_HEADS * DIL_C]
C_OUT = [C_MEM[0] + MEM_HEADS * MEM_C]
C_LR = C_OUT[0] + KC
C_GLA = C_LR + 1
C_MEM.append(C_GLA + GLA_HEADS * GLA_C)
C_OUT.append(C_MEM[1] + MEM_HEADS * MEM_C)
C_END = C_OUT[1] + KC


def need(engine, semaphore, count):
    if not isinstance(count, int) or count > 0:
        engine.wait_ge(semaphore, count)


def halves(j0, per, h, c):
    return (per // 2) * h + (j0 + c) // 2


def root_start(act, out, var, var_done, root, m):
    act.wait_ge(var_done, m + 1)
    act.activation(out, var, ACT.Ln).then_inc(root, 1)
    act.wait_ge(root, 2 * m + 1)
    act.activation(out, out, ACT.Exp, scale=-0.5).then_inc(root, 1)


def root_refine(dve, r, var, tmp, root, step, m):
    dve.wait_ge(root, 2 * m + 2)
    dve.tensor_tensor(tmp, r, r, ALU.mult).then_inc(step, 1)
    dve.wait_ge(step, 4 * m + 1)
    dve.tensor_tensor(tmp, tmp, var, ALU.mult).then_inc(step, 1)
    dve.wait_ge(step, 4 * m + 2)
    dve.tensor_scalar(tmp, tmp, -0.5, 1.5, ALU.mult, ALU.add).then_inc(step, 1)
    dve.wait_ge(step, 4 * m + 3)
    dve.tensor_tensor(r, r, tmp, ALU.mult).then_inc(step, 1)


def build(nc, A):
    with ExitStack() as top:
        def sb(name, shape, dt=F32, stack=top):
            return stack.enter_context(nc.sbuf_tensor(name, shape, dt))

        def sem(name):
            return top.enter_context(nc.semaphore(name))

        def scratch(name, shape):
            return nc.dram_tensor(name, shape, F32, kind="Internal").ap()

        top.enter_context(nc.allow_non_contiguous_dma(reason="gains and biases as columns, once"))

        xt_scratch = scratch("xt_scratch", (P, KC, TOK))
        mt_scratch = scratch("mt_scratch", (P, KC, MT))
        y_scratch = [scratch(f"y_scratch{i}", (FC, P, TOK)) for i in range(2)]

        def ps(name, n):
            return top.enter_context(nc.psum_tensor(name, [P, n], F32))

        z_ps = [ps("z_ps0", 512), ps("z_ps1", 512)]
        s_ps = ps("s_ps", 1024)
        t_ps = ps("t_ps", 1024)
        o_ps = ps("o_ps", 512)
        v_ps = ps("v_ps", 512)

        ident = sb("ident", [P, P])
        ones = sb("ones", [P, P])
        gains = sb("gains", [P, 5, KC])
        onorm = sb("onorm", [P, 2])

        w_raw = [sb(f"w_raw{i}", [P, FC, P]) for i in range(2)]
        w_hi = [sb(f"w_hi{i}", [P, FC, P], F32R) for i in range(2)]
        w_lo = [sb(f"w_lo{i}", [P, FC, P], F32R) for i in range(2)]
        ring_in = [sem("ring_in0"), sem("ring_in1")]
        hi_done, lo_done = sem("hi_done"), sem("lo_done")
        z_ready = [sem("z_ready0"), sem("z_ready1")]
        z_free = [sem("z_free0"), sem("z_free1")]
        sum_done, var_done, root, step = (sem("norm_" + n) for n in ("sum_done", "var_done", "root", "step"))
        x_stored = sem("x_stored")
        ident_in, const_in, aux_in = sem("ident_in"), sem("const_in"), sem("aux_in")

        def w_view(w, col):
            return w.rearrange("(k p) c -> p k c", p=P)[:, :, bass.ds(col, P)]

        def w_load(sp, w, col, slot, j, nk=KC):
            columns = w_view(w, col)
            need(sp, lo_done, j - 1)
            sp.dma_start(w_raw[slot][:, 0:nk, :], columns).then_inc(ring_in[slot], 16)

        def split_hi(act, j, j_half, slot, nk=KC):
            act.wait_ge(ring_in[slot], 16 * j_half + 16)
            need(act, z_ready[1], j - 1)
            act.activation(w_hi[slot][:, 0:nk, :], w_raw[slot][:, 0:nk, :], ACT.Copy).then_inc(hi_done, 1)

        def split_lo(dve, j, slot, nk=KC):
            dve.wait_ge(hi_done, j + 1)
            dve.tensor_tensor(w_lo[slot][:, 0:nk, :], w_raw[slot][:, 0:nk, :],
                              w_hi[slot][:, 0:nk, :].bitcast(F32), ALU.subtract).then_inc(lo_done, 1)

        def unit(pe, j, slot, s, hi, lo, width=SEQ, nk=KC):
            if s == 0:
                pe.wait_ge(lo_done, j + 1)
            need(pe, z_free[s], j)
            tok = slice(s * width, (s + 1) * width)
            if not isinstance(hi, list):
                hi, lo = [hi[:, k, :] for k in range(nk)], [lo[:, k, :] for k in range(nk)]
            for k in range(nk):
                pe.matmul(z_ps[s][:, 0:width], w_hi[slot][:, k, :], hi[k][:, tok], start=(k == 0), stop=False)
                pe.matmul(z_ps[s][:, 0:width], w_hi[slot][:, k, :], lo[k][:, tok], start=False, stop=False)
                mm = pe.matmul(z_ps[s][:, 0:width], w_lo[slot][:, k, :], hi[k][:, tok], start=False,
                               stop=(k == nk - 1))
            mm.then_inc(z_ready[s], 1)

        def silu_pair(act, j, outs):
            for s in range(NS):
                act.wait_ge(z_ready[s], j + 1)
                act.activation(outs[s], z_ps[s][:], ACT.Silu).then_inc(z_free[s], 1)

        def carrier(dve):
            dve.tensor_copy(cell[1][:], cell[0][:])

        def load_and_transpose(xt0, mt0, st):
            if True:
                rows = [sb(f"rows{i}", [P, D], stack=st) for i in range(2)]
                sq = [sb(f"msq{i}", [P, MT], stack=st) for i in range(2)]
                msd, mvar, mtmp = (sb(n, [P, MT], stack=st) for n in ("msd", "mvar", "mtmp"))
                row_in = [sem("row_in0"), sem("row_in1")]
                turned, moved = sem("rows_turned"), [sem("rows_moved0"), sem("rows_moved1")]
                m_sq, m_sum, m_hat = sem("m_sq"), sem("m_sum"), sem("m_hat")
                N = NT + MT // P
                NM = MT // P
                srcs = [(A[n][0], i) for n in ("mem_prompt", "mem_sample") for i in range(NMEM // P)]
                srcs += [(A[n][0], i) for n in ("x_prompt", "x_sample") for i in range(SEQ // P)]
                block = st.enter_context(nc.Block())

                @block.sync
                def _(sp):
                    sp.dma_start(ident[:], A["c_ident"]).then_inc(ident_in, 16)
                    for t, (a, i) in enumerate(srcs):
                        need(sp, turned, t - 1)
                        sp.dma_start(rows[t % 2][:], a[i * P:(i + 1) * P, :]).then_inc(row_in[t % 2], 16)
                    w_load(sp, A["a_win"][0], 0, 0, 0)
                    for b in range(2):
                        sp.wait_ge(moved[b], N)
                    sp.dma_start(xt_scratch, xt0[:]).then_inc(x_stored, 16)
                    sp.wait_ge(m_hat, KC)
                    sp.dma_start(mt_scratch, mt0[:]).then_inc(x_stored, 16)

                @block.gpsimd
                def _(pool):
                    pool.memset(ones[:], 1.0).then_inc(aux_in, 1)
                    pool.memset(half_col[:], 0.5)
                    pool.memset(cell[0][:], 0.0).then_inc(aux_in, 1)
                    for i, n in enumerate(("a_ln", "a_mln", "b_ln", "b_mln", "lnf")):
                        g = A[n] if n == "lnf" else A[n][0]
                        pool.dma_start(gains[:, i, :], g.rearrange("(k p) -> p k", p=P)).then_inc(const_in, 16)
                    pool.dma_start(onorm[:], A["b_onorm"][0].rearrange("(k p) -> p k", p=P)).then_inc(const_in, 16)

                @block.tensor
                def _(pe):
                    pe.wait_ge(ident_in, 16)
                    pe.wait_ge(aux_in, 1)

                    def sum_squares(k):
                        pe.wait_ge(m_sq, k + 1)
                        pe.matmul(o_ps[:], ones[:], sq[k % 2][:], start=(k == 0), stop=(k == KC - 1)).then_inc(m_sum, 1)
                    for t in range(N):
                        pe.wait_ge(row_in[t % 2], 16 * (t // 2) + 16)
                        for b in range(2):
                            need(pe, moved[b], t - 1)
                        dst = (s_ps, t_ps)[t % 2]
                        for k in range(KC):
                            tr = pe.transpose(dst[:, k * P:(k + 1) * P], rows[t % 2][:, k * P:(k + 1) * P], ident[:])
                        tr.then_inc(turned, 1)
                        if t > NM:
                            sum_squares(t - NM - 1)
                    sum_squares(KC - 1)

                def evac(eng, copy, t, half):
                    eng.wait_ge(turned, t + 1)
                    src = (s_ps, t_ps)[t % 2][:, half * 512:(half + 1) * 512].rearrange("p (k i) -> p k i", k=4)
                    out = mt0[:, 4 * half:4 * half + 4, t * P:(t + 1) * P] if t < NM else \
                        xt0[:, 4 * half:4 * half + 4, (t - NM) * P:(t - NM + 1) * P]
                    copy(out, src).then_inc(moved[half], 1)

                @block.scalar
                def _(act):
                    for t in range(N):
                        evac(act, lambda o, i: act.activation(o, i, ACT.Copy), t, 0)
                        if t < NM:
                            continue
                        k = t - NM
                        if k == 0:
                            for b in range(2):
                                act.wait_ge(moved[b], NM)
                        need(act, m_sum, k - 1)
                        act.activation(sq[k % 2][:], mt0[:, k, :], ACT.Square).then_inc(m_sq, 1)
                    act.preload_act_table_set("natural_log_exp_and_others")
                    root_start(act, msd[:], mvar[:], var_done, root, 0)

                @block.vector
                def _(dve):
                    dve.memset(eps_col[:], EPS).then_inc(eps_set, 1)
                    for t in range(N):
                        evac(dve, lambda o, i: dve.tensor_copy(o, i), t, 1)
                    dve.wait_ge(m_sum, KC)
                    dve.tensor_scalar(mvar[:], o_ps[:], 1.0 / D, EPS, ALU.mult, ALU.add).then_inc(var_done, 1)
                    root_refine(dve, msd[:], mvar[:], mtmp[:], root, step, 0)
                    dve.wait_ge(step, 4)
                    for k in range(KC):
                        dve.tensor_tensor(mt0[:, k, :], mt0[:, k, :], msd[:], ALU.mult).then_inc(m_hat, 1)

        eps_col, half_col = sb("eps_col", [P, 1]), sb("half_col", [P, 1])
        cell = [sb("cell0", [P, 1]), sb("cell1", [P, 1])]
        eps_set = sem("eps_set")

        def norm_split(tag, xT, acc, summed, gain, hi, lo, permuted, first_chunk, second, stores, st):
            NB, N = 4, NS * KC
            rstd, var = sb(f"{tag}_rstd", [P, TOK], stack=st), sb(f"{tag}_var", [P, TOK], stack=st)
            tmp = [sb(f"{tag}_tmp{i}", [P, SEQ], stack=st) for i in range(NS)]
            h = [sb(f"{tag}_h{i}", [P, SEQ], stack=st) for i in range(NB)]
            M0 = 3 if summed else 1
            h_done, hh_done, hl_pool, hl_dve = (sem(f"{tag}_{n}") for n in ("h_done", "hh_done", "hl_pool", "hl_dve"))
            if not summed:
                sq = [sb(f"{tag}_sq{i}", [P, TOK], stack=st) for i in range(2)]
                sq_done, acc_done = sem(f"{tag}_sq_done"), sem(f"{tag}_acc_done")
            block = st.enter_context(nc.Block())
            banks = (o_ps, v_ps)
            toks = [slice(s * SEQ, (s + 1) * SEQ) for s in range(NS)]

            def on_dve(n):
                return n % 4 == 3

            def low_part_done(eng, n):
                if on_dve(n):
                    eng.wait_ge(hl_dve, (n + 1) // 4)
                else:
                    eng.wait_ge(hl_pool, n + 1 - (n + 1) // 4)

            def low_part(eng, n):
                k, s = n // NS, n % NS
                eng.wait_ge(hh_done, n + 1)
                return eng.tensor_tensor(lo[:, k, toks[s]], h[n % NB][:], hi[:, k, toks[s]].bitcast(F32), ALU.subtract)

            @block.sync
            def _(sp):
                w_load(sp, *second, (first_chunk + 1) % 2, first_chunk + 1)
                sp.wait_ge(x_stored, 16 * stores)

            @block.scalar
            def _(act):
                act.preload_act_table_set("natural_log_exp_and_others")
                if not summed:
                    for k in range(KC):
                        need(act, acc_done, k - 2)
                        act.activation(acc[:] if k == 0 else sq[k % 2][:], xT[:, k, :], ACT.Square).then_inc(sq_done, 1)
                split_hi(act, first_chunk, first_chunk // 2, first_chunk % 2)
                for s in range(NS):
                    root_start(act, rstd[:, toks[s]], var[:, toks[s]], var_done, root, M0 + s)
                for n in range(N):
                    k, s = n // NS, n % NS
                    act.wait_ge(h_done, n + 1)
                    act.activation(hi[:, k, toks[s]], h[n % NB][:], ACT.Copy).then_inc(hh_done, 1)

            @block.tensor
            def _(pe):
                if not summed:
                    pe.wait_ge(acc_done, KC - 1)
                for s in range(NS):
                    pe.matmul(banks[s][:], ones[:], acc[:, toks[s]], start=True, stop=True).then_inc(sum_done, 1)
                pe.wait_ge(lo_done, first_chunk + 1)
                for s in range(NS):
                    need(pe, z_free[s], first_chunk)
                slot = first_chunk % 2
                for n in range(N):
                    k, s = n // NS, n % NS
                    low_part_done(pe, n)
                    pe.matmul(z_ps[s][:], w_hi[slot][:, k, :], hi[:, k, toks[s]], start=(k == 0), stop=False)
                    pe.matmul(z_ps[s][:], w_hi[slot][:, k, :], lo[:, k, toks[s]], start=False, stop=False)
                    mm = pe.matmul(z_ps[s][:], w_lo[slot][:, k, :], hi[:, k, toks[s]], start=False, stop=(k == KC - 1))
                    if k == KC - 1:
                        mm.then_inc(z_ready[s], 1)

            @block.vector
            def _(dve):
                dve.wait_ge(const_in, 16 * 6)
                if not summed:
                    for k in range(1, KC):
                        dve.wait_ge(sq_done, k + 1)
                        need(dve, acc_done, k - 1)
                        dve.tensor_tensor(acc[:], acc[:], sq[k % 2][:], ALU.add).then_inc(acc_done, 1)
                split_lo(dve, first_chunk, first_chunk % 2)
                for s in range(NS):
                    dve.wait_ge(sum_done, M0 + s)
                    dve.tensor_scalar(var[:, toks[s]], banks[s][:], 1.0 / D, EPS, ALU.mult, ALU.add).then_inc(var_done, 1)
                for s in range(NS):
                    root_refine(dve, rstd[:, toks[s]], var[:, toks[s]], tmp[s][:], root, step, M0 + s)
                dve.wait_ge(step, 4 * (M0 + NS))
                for n in range(N + 2):
                    if n < N:
                        k, s = n // NS, n % NS
                        if n >= NB:
                            low_part_done(dve, n - NB)
                        out, x, r = h[n % NB][:], xT[:, k, toks[s]], rstd[:, toks[s]]
                        if permuted:
                            out = out.rearrange("p (r i) -> p i r", r=RES)
                            x, r = (a.rearrange("p (i r) -> p i r", r=RES) for a in (x, r))
                        dve.scalar_tensor_tensor(out=out, in0=x, scalar=gains[:, gain, k:k + 1], in1=r,
                                                 op0=ALU.mult, op1=ALU.mult).then_inc(h_done, 1)
                    if n >= 2 and on_dve(n - 2):
                        low_part(dve, n - 2).then_inc(hl_dve, 1)

            @block.gpsimd
            def _(pool):
                for n in range(N):
                    if not on_dve(n):
                        low_part(pool, n).then_inc(hl_pool, 1)

        def dilated(hi, lo):
            with ExitStack() as st:
                qk = sb("qk", [P, 2 * NG, TOK], stack=st)
                vT = sb("vT", [P, TOK], stack=st)
                v = sb("v", [P, NG, NT, HD], stack=st)
                bias = sb("bias", [P, RES, KEYS], stack=st)
                x = [sb(f"x{i}", [P, KEYS], stack=st) for i in range(2)]
                pT = [sb(f"pT{i}", [P, 6, SEQ], stack=st) for i in range(NS)]
                gate = sb("gate", [P, TOK], stack=st)
                y = sb("y", [P, TOK], stack=st)
                mx, nm, l, rl = (sb(n, [P, 2], stack=st) for n in ("mx", "nm", "l", "rl"))
                (bias_in, bias_ready, qk_done, max_done, neg_done, exp_done, rl_done, p_ready, tr_done, pt_ready,
                 vtr_done, v_ready, pv_done, y_done, y_stored) = (sem("dil_" + n) for n in (
                     "bias_in", "bias_ready", "qk_done", "max_done", "neg_done", "exp_done", "rl_done", "p_ready",
                     "tr_done", "pt_ready", "vtr_done", "v_ready", "pv_done", "y_done", "y_stored"))
                w = A["a_win"][0]
                TPS = SEQ // P
                V0, G = 2 * NG, DIL_C - 1
                QK0 = 2 * V0
                block = st.enter_context(nc.Block())

                def col(h, c):
                    if c < V0:
                        return 3 * (c // 2) * DIL_W + (c % 2) * DIL_W + h * HD
                    if c < G:
                        return 3 * (c - V0) * DIL_W + 2 * DIL_W + h * HD
                    return GATE_A + h * HD

                @block.sync
                def _(sp):
                    def head(h, start=0, stop=DIL_C):
                        for c in range(start, stop):
                            w_load(sp, w, col(h, c), c % 2, C_DIL + DIL_C * h + c)
                    sp.dma_start(bias[:], A["c_bias"]).then_inc(bias_in, 16)
                    head(0, start=2)
                    with sp.Fori(1, DIL_HEADS) as h:
                        head(h)
                    w_load(sp, w, QKV_A, C_MEM[0] % 2, C_MEM[0])

                @block.gpsimd
                def _(pool):
                    def head(h, more):
                        if more:
                            pool.wait_ge(max_done, NT * h + NT)
                            pool.tensor_tensor(bias[:].rearrange("p r k -> p (r k)"), bias[:].rearrange("p r k -> p (r k)"),
                                               half_col[:].to_broadcast([P, RES * KEYS]), ALU.mult).then_inc(bias_ready, 1)
                        pool.wait_ge(y_done, NS * h + NS)
                        pool.dma_start(y_scratch[0][h], y[:]).then_inc(y_stored, 16)
                    head(0, True)
                    with pool.Fori(1, DIL_HEADS - 1) as h:
                        head(h, True)
                    head(DIL_HEADS - 1, False)
                    pool.wait_ge(y_stored, 16 * DIL_HEADS)

                @block.tensor
                def _(pe):
                    def scores(h, t):
                        s, r = t // TPS, t % TPS
                        T = NT * h + t
                        need(pe, max_done, T)
                        if t == 0:
                            need(pe, y_done, NS * h)
                            pe.wait_ge(z_free[1], C_DIL + DIL_C * h + V0)
                            pe.wait_ge(z_free[0], C_DIL + DIL_C * h + V0)
                        q = slice(s * SEQ + r * P, s * SEQ + (r + 1) * P)
                        pe.matmul(s_ps[:, 0:SEQ], qk[:, 0, q], qk[:, 1, s * SEQ:(s + 1) * SEQ], start=True, stop=True)
                        pe.matmul(s_ps[:, SEQ:SEQ + P], qk[:, 2, q], qk[:, 3, q], start=True, stop=True)
                        pe.matmul(s_ps[:, SEQ + P:KEYS], qk[:, 4, q], qk[:, 5, q], start=True, stop=True).then_inc(qk_done, 1)

                    def turn_probs(h, t):
                        T = NT * h + t
                        pe.wait_ge(p_ready, T + 1)
                        need(pe, pt_ready, T)
                        for c in range(KEYS // P):
                            tr = pe.transpose(t_ps[:, c * P:(c + 1) * P], x[t % 2][:, c * P:(c + 1) * P], ident[:])
                        tr.then_inc(tr_done, 1)

                    def turn_values(h, g, s):
                        n = NG * NS * h + NS * g + s
                        pe.wait_ge(z_free[s], C_DIL + DIL_C * h + V0 + g + 1)
                        need(pe, v_ready, n)
                        for i in range(TPS):
                            tr = pe.transpose(v_ps[:, i * P:(i + 1) * P],
                                              vT[:, s * SEQ + i * P:s * SEQ + (i + 1) * P], ident[:])
                        tr.then_inc(vtr_done, 1)

                    def weighted_values(h, s):
                        pe.wait_ge(pt_ready, NT * h + TPS * (s + 1))
                        pe.wait_ge(v_ready, NG * NS * (h + 1))
                        if s == 1:
                            pe.wait_ge(y_done, NS * h + 1)
                        for kt in range(TPS):
                            pe.matmul(o_ps[:], v[:, 0, s * TPS + kt, :], pT[s][:, kt, :], start=(kt == 0), stop=False,
                                      skip_group_check=True)
                        for r in range(TPS):
                            for g in (1, 2):
                                mm = pe.matmul(o_ps[:, r * P:(r + 1) * P], v[:, g, s * TPS + r, :],
                                               pT[s][:, TPS - 1 + g, r * P:(r + 1) * P], start=False,
                                               stop=(r == TPS - 1 and g == 2), skip_group_check=True)
                        mm.then_inc(pv_done, 1)

                    def rest(h, n):
                        if n in (0, 1):
                            turn_probs(h, NT - 2 + n)
                        if n == 0:
                            weighted_values(h, 0)
                        if n == 3:
                            weighted_values(h, 1)

                    def head(h, before):
                        for n in range(2 * DIL_C):
                            if before is not None or n >= NS:
                                unit(pe, C_DIL + DIL_C * h + n // 2, (n // 2) % 2, n % 2, hi, lo)
                            if before is not None:
                                rest(before, n)
                            if 0 <= n - 2 * V0 - 1 < NG * NS:
                                turn_values(h, (n - 2 * V0 - 1) // 2, (n - 2 * V0 - 1) % 2)
                            if n >= QK0:
                                scores(h, n - QK0)
                            if n >= QK0 + 2:
                                turn_probs(h, n - QK0 - 2)
                    head(0, None)
                    with pe.Fori(1, DIL_HEADS) as h:
                        head(h, h - 1)
                    for n in range(4):
                        rest(DIL_HEADS - 1, n)

                @block.scalar
                def _(act):
                    def exps(h, t):
                        T = NT * h + t
                        act.wait_ge(neg_done, T + 1)
                        act.activation(x[t % 2][:], x[t % 2][:], ACT.Exp, bias=nm[:, t % 2:t % 2 + 1],
                                       accum_out=l[:, t % 2:t % 2 + 1]).then_inc(exp_done, 1)

                    def move_probs(h, t):
                        s, r = t // TPS, t % TPS
                        act.wait_ge(tr_done, NT * h + t + 1)
                        if t == 0:
                            need(act, pv_done, NS * h)
                        act.activation(pT[s][:, :, r * P:(r + 1) * P],
                                       t_ps[:, 0:KEYS].rearrange("p (c q) -> p c q", q=P), ACT.Copy).then_inc(pt_ready, 1)

                    def move(h, n):
                        c, s = n // 2, n % 2
                        j = C_DIL + DIL_C * h + c
                        tok = slice(s * SEQ, (s + 1) * SEQ)
                        if c == G:
                            if s == 1:
                                need(act, y_done, NS * h)
                                silu_pair(act, j, [gate[:, 0:SEQ], gate[:, SEQ:TOK]])
                            return
                        act.wait_ge(z_ready[s], j + 1)
                        if n == 0:
                            need(act, qk_done, NT * h)
                        if c >= V0:
                            need(act, vtr_done, NG * NS * h + NS * (c - V0) + s - 1)
                        out = qk[:, c, tok] if c < V0 else vT[:, tok]
                        act.activation(out, z_ps[s][:], ACT.Copy).then_inc(z_free[s], 1)

                    def rest(h, n):
                        if n == 0:
                            move_probs(h, NT - 3)
                            exps(h, NT - 1)
                        if n in (1, 2):
                            move_probs(h, NT - 3 + n)

                    def head(h, before):
                        for n in range(2 * DIL_C):
                            c = n // 2
                            if n % 2 == 0:
                                j = C_DIL + DIL_C * h + c + 1
                                split_hi(act, j, halves(C_DIL, DIL_C, h, c + 1), (c + 1) % 2)
                            if before is not None:
                                rest(before, n)
                            if n >= QK0 + 1:
                                exps(h, n - QK0 - 1)
                            if n >= QK0 + 3:
                                move_probs(h, n - QK0 - 3)
                            move(h, n)
                    act.preload_act_table(ACT.Exp)
                    head(0, None)
                    with act.Fori(1, DIL_HEADS) as h:
                        head(h, h - 1)
                    for n in range(3):
                        rest(DIL_HEADS - 1, n)

                @block.vector
                def _(dve):
                    def softmax_in(h, t):
                        T = NT * h + t
                        b = t % 2
                        dve.wait_ge(qk_done, T + 1)
                        need(dve, tr_done, T - 1)
                        if t == 0:
                            dve.wait_ge(bias_in, 16)
                            need(dve, bias_ready, h)
                        carrier(dve)
                        dve.tensor_tensor_reduce(x[b][:], s_ps[:, 0:KEYS], bias[:, t % TPS, :], SCALE, -3e38,
                                                 ALU.add, ALU.max, mx[:, b:b + 1]).then_inc(max_done, 1)
                        dve.wait_ge(max_done, T + 1)
                        dve.tensor_scalar(nm[:, b:b + 1], mx[:, b:b + 1], -1.0, None, ALU.mult).then_inc(neg_done, 1)

                    def softmax_out(h, t):
                        T = NT * h + t
                        b = t % 2
                        dve.wait_ge(exp_done, T + 1)
                        dve.reciprocal(rl[:, b:b + 1], l[:, b:b + 1]).then_inc(rl_done, 1)
                        dve.wait_ge(rl_done, T + 1)
                        dve.tensor_scalar(x[b][:], x[b][:], rl[:, b:b + 1], None, ALU.mult).then_inc(p_ready, 1)

                    def move_values(h, m):
                        n = NG * NS * h + m
                        g, s = m // NS, m % NS
                        dve.wait_ge(vtr_done, n + 1)
                        if m == 0:
                            need(dve, pv_done, NS * h)
                        dve.tensor_copy(v[:, g, s * TPS:(s + 1) * TPS, :],
                                        v_ps[:].rearrange("p (t e) -> p t e", e=HD)).then_inc(v_ready, 1)

                    def finish(h, s):
                        dve.wait_ge(pv_done, NS * h + s + 1)
                        if s == 0:
                            for b in range(NS):
                                dve.wait_ge(z_free[b], C_DIL + DIL_C * h + G + 1)
                        tok = slice(s * SEQ, (s + 1) * SEQ)
                        dve.tensor_tensor(y[:, tok].rearrange("p (i r) -> p r i", r=RES),
                                          o_ps[:].rearrange("p (r i) -> p r i", r=RES),
                                          gate[:, tok].rearrange("p (r i) -> p r i", r=RES), ALU.mult).then_inc(y_done, 1)

                    def rest(h, n):
                        if n == 0:
                            softmax_out(h, NT - 1)
                        if n == 1:
                            finish(h, 0)
                        if n == 4:
                            finish(h, 1)

                    def head(h, before):
                        for n in range(2 * DIL_C):
                            c = n // 2
                            if n % 2 == 0:
                                split_lo(dve, C_DIL + DIL_C * h + c + 1, (c + 1) % 2)
                            if before is not None and n == 0:
                                softmax_in(before, NT - 1)
                            if n >= QK0 + 1:
                                softmax_in(h, n - QK0 - 1)
                            if 0 <= n - 2 * V0 - 2 < NG * NS:
                                move_values(h, n - 2 * V0 - 2)
                            if n >= QK0 + 1:
                                softmax_out(h, n - QK0 - 1)
                            if before is not None:
                                rest(before, n)
                            if n == 2 * G:
                                need(dve, y_stored, 16 * h)
                    head(0, None)
                    with dve.Fori(1, DIL_HEADS) as h:
                        head(h, h - 1)
                    softmax_in(DIL_HEADS - 1, NT - 1)
                    for n in range(5):
                        rest(DIL_HEADS - 1, n)

        def memory(i, hi, lo):
            tag = "ab"[i]
            with ExitStack() as st:
                m_hat = sb(tag + "m_hat", [P, KC, MT], stack=st)
                m_g = [sb(f"{tag}m_g{b}", [P, MT], stack=st) for b in range(2)]
                m_hi = sb(tag + "m_hi", [P, KC, MT], F32R, stack=st)
                m_lo = sb(tag + "m_lo", [P, KC, MT], F32R, stack=st)
                kT = sb(tag + "kT", [P, MT], stack=st)
                vT = sb(tag + "vmT", [P, MT], stack=st)
                v = sb(tag + "vm", [P, MT // P, HD], stack=st)
                q = sb(tag + "qm", [P, TOK], stack=st)
                gate = sb(tag + "gm", [P, TOK], stack=st)
                y = sb(tag + "ym", [P, TOK], stack=st)
                p = [sb(f"{tag}pm{b}", [P, 2, NMEM], stack=st) for b in range(2)]
                pT = [sb(f"{tag}pmT{s}", [P, 2, SEQ], stack=st) for s in range(NS)]
                mx, nm, l, rl = (sb(tag + n, [P, 2, 2], stack=st) for n in ("mxm", "nmm", "lm", "rlm"))
                mh_in = [sem(f"{tag}mem_mh_in{b}") for b in range(2)]
                (mg_done, mh_done, ml_done, qk_done, max_done, neg_done, exp_done, rl_done, p_ready, tr_done,
                 pt_ready, vtr_done, v_ready, pv_done, y_done, y_stored) = (sem(f"{tag}mem_" + n) for n in (
                     "mg_done", "mh_done", "ml_done", "qk_done", "max_done", "neg_done", "exp_done", "rl_done",
                     "p_ready", "tr_done", "pt_ready", "vtr_done", "v_ready", "pv_done", "y_done", "y_stored"))
                wm, w = A["ab"[i] + "_wmem"][0], A["ab"[i] + "_win"][0]
                q_col = QKV_A if i == 0 else GQM
                gate_col = (GATE_A if i == 0 else GATE_B) + (BRANCH - MEM_W)
                C0 = C_MEM[i]
                NP = 4
                Q, K, V, G = range(MEM_C)
                nxt = (A["a_wout"][0], FC) if i == 0 else (A["b_wout"][0], FC)
                block = st.enter_context(nc.Block())

                @block.sync
                def _(sp):
                    for b in range(2):
                        ks = slice(b * KC // 2, (b + 1) * KC // 2)
                        sp.dma_start(m_hat[:, ks, :], mt_scratch[:, ks, :]).then_inc(mh_in[b], 16)

                    def head(h, start=0):
                        cols = [(w, q_col + h * HD), (wm, (h - 1) * HD + HD), (wm, MEM_W + h * HD), (w, gate_col + h * HD)]
                        for c in range(start, MEM_C):
                            w_load(sp, *cols[c], (C0 + c) % 2, C0 + MEM_C * h + c)
                    head(0, start=1)
                    with sp.Fori(1, MEM_HEADS) as h:
                        head(h)
                    for b in range(2):
                        w_load(sp, nxt[0], b * P, (C_OUT[i] + b) % 2, C_OUT[i] + b, nk=FC)

                @block.gpsimd
                def _(pool):
                    def head(h):
                        pool.wait_ge(y_done, NS * h + NS)
                        pool.dma_start(y_scratch[i][h + (FC - MEM_HEADS)], y[:]).then_inc(y_stored, 16)
                    head(0)
                    with pool.Fori(1, MEM_HEADS) as h:
                        head(h)
                    pool.wait_ge(y_stored, 16 * MEM_HEADS)

                @block.tensor
                def _(pe):
                    def scores(h, p_):
                        N = NP * h + p_
                        need(pe, exp_done, 2 * N - 2)
                        if p_ == 0:
                            need(pe, y_done, NS * h)
                        pe.wait_ge(z_free[p_ // 2], C0 + MEM_C * h + K + 1)
                        s = p_ // 2
                        for t in range(2):
                            tok = s * SEQ + (2 * (p_ % 2) + t) * P
                            mm = pe.matmul(s_ps[:, (p_ % 2) * 512 + t * NMEM:(p_ % 2) * 512 + (t + 1) * NMEM],
                                           q[:, tok:tok + P], kT[:, s * NMEM:(s + 1) * NMEM], start=True, stop=True)
                        mm.then_inc(qk_done, 1)

                    def turn_probs(h, p_):
                        N = NP * h + p_
                        pe.wait_ge(p_ready, 2 * N + 2)
                        need(pe, pt_ready, N - 1)
                        for m in range(2):
                            for t in range(2):
                                o = (p_ % 2) * 512 + m * 256 + t * P
                                tr = pe.transpose(t_ps[:, o:o + P], p[p_ % 2][:, t, m * P:(m + 1) * P], ident[:])
                        tr.then_inc(tr_done, 1)

                    def turn_values(h):
                        pe.wait_ge(z_free[0], C0 + MEM_C * h + V + 1)
                        pe.wait_ge(z_free[1], C0 + MEM_C * h + V + 1)
                        for m in range(MT // P):
                            tr = pe.transpose(v_ps[:, m * P:(m + 1) * P], vT[:, m * P:(m + 1) * P], ident[:])
                        tr.then_inc(vtr_done, 1)

                    def weighted_values(h, s):
                        pe.wait_ge(pt_ready, NP * h + 2 * s + 2)
                        pe.wait_ge(v_ready, h + 1)
                        if s == 1:
                            pe.wait_ge(y_done, NS * h + 1)
                        for m in range(2):
                            mm = pe.matmul(o_ps[:], v[:, 2 * s + m, :], pT[s][:, m, :], start=(m == 0), stop=(m == 1))
                        mm.then_inc(pv_done, 1)

                    def rest(h, n):
                        if n == 0:
                            turn_probs(h, 2)
                        if n == 1:
                            weighted_values(h, 0)
                            turn_probs(h, 3)
                        if n == 3:
                            weighted_values(h, 1)

                    def head(h, before):
                        for n in range(2 * MEM_C):
                            c = n // 2
                            if before is None and c == K:
                                pe.wait_ge(ml_done, KC)
                            a, b, width = (m_hi, m_lo, NMEM) if c in (K, V) else (hi, lo, SEQ)
                            unit(pe, C0 + MEM_C * h + c, (C0 + c) % 2, n % 2, a, b, width=width)
                            if before is not None:
                                rest(before, n)
                            if n == 4:
                                scores(h, 0)
                                scores(h, 1)
                            if n == 6:
                                turn_values(h)
                                turn_probs(h, 0)
                                scores(h, 2)
                            if n == 7:
                                turn_probs(h, 1)
                                scores(h, 3)
                    head(0, None)
                    with pe.Fori(1, MEM_HEADS) as h:
                        head(h, h - 1)
                    for n in range(4):
                        rest(MEM_HEADS - 1, n)

                @block.scalar
                def _(act):
                    def exps(h, p_):
                        N = NP * h + p_
                        b = p_ % 2
                        act.wait_ge(neg_done, N + 1)
                        need(act, tr_done, N - 1)
                        for t in range(2):
                            act.activation(p[b][:, t, :], s_ps[:, b * 512 + t * NMEM:b * 512 + (t + 1) * NMEM], ACT.Exp,
                                           bias=nm[:, b, t:t + 1], scale=SCALE, accum_out=l[:, b, t:t + 1])\
                                .then_inc(exp_done, 1)

                    def move_probs(h, p_):
                        N = NP * h + p_
                        s, b = p_ // 2, p_ % 2
                        act.wait_ge(tr_done, N + 1)
                        if p_ == 0:
                            need(act, pv_done, NS * h)
                        act.activation(pT[s][:, :, b * 256:(b + 1) * 256],
                                       t_ps[:, b * 512:(b + 1) * 512].rearrange("p (m q) -> p m q", q=256),
                                       ACT.Copy).then_inc(pt_ready, 1)

                    def move(h, n):
                        c, s = n // 2, n % 2
                        j = C0 + MEM_C * h + c
                        if c == G:
                            if s == 1:
                                need(act, y_done, NS * h)
                                silu_pair(act, j, [gate[:, 0:SEQ], gate[:, SEQ:TOK]])
                            return
                        act.wait_ge(z_ready[s], j + 1)
                        if n == 0:
                            need(act, qk_done, NP * h)
                        if c == V:
                            need(act, vtr_done, h)
                        if c == Q:
                            out, src = q[:, s * SEQ:(s + 1) * SEQ], z_ps[s][:]
                        else:
                            out, src = (kT if c == K else vT)[:, s * NMEM:(s + 1) * NMEM], z_ps[s][:, 0:NMEM]
                        act.activation(out, src, ACT.Copy).then_inc(z_free[s], 1)

                    def rest(h, n):
                        if n == 0:
                            exps(h, 2)
                            move_probs(h, 1)
                            exps(h, 3)
                        if n == 1:
                            move_probs(h, 2)
                        if n == 2:
                            move_probs(h, 3)

                    def head(h, before, last):
                        for n in range(2 * MEM_C):
                            c = n // 2
                            if n % 2 == 0:
                                ahead = C0 + MEM_C * h + c + 1
                                split_hi(act, ahead, halves(C0, MEM_C, h, c + 1), (C0 + c + 1) % 2,
                                         nk=FC if last and c == MEM_C - 1 else KC)
                            if before is not None:
                                rest(before, n)
                            if before is None and n < 2:
                                for k in range(n * KC // 2, (n + 1) * KC // 2):
                                    act.wait_ge(mg_done, k + 1)
                                    act.activation(m_hi[:, k, :], m_g[k % 2][:], ACT.Copy).then_inc(mh_done, 1)
                            if n == 5:
                                exps(h, 0)
                                exps(h, 1)
                            if n == 7:
                                move_probs(h, 0)
                            move(h, n)
                    act.preload_act_table(ACT.Exp)
                    head(0, None, False)
                    with act.Fori(1, MEM_HEADS - 1) as h:
                        head(h, h - 1, False)
                    head(MEM_HEADS - 1, MEM_HEADS - 2, True)
                    for n in range(3):
                        rest(MEM_HEADS - 1, n)

                @block.vector
                def _(dve):
                    def softmax_in(h, p_):
                        N = NP * h + p_
                        b = p_ % 2
                        dve.wait_ge(qk_done, N + 1)
                        dve.tensor_reduce(mx[:, b, :], s_ps[:, b * 512:(b + 1) * 512].rearrange("p (t m) -> p t m", t=2),
                                          AX, ALU.max).then_inc(max_done, 1)
                        dve.wait_ge(max_done, N + 1)
                        dve.tensor_scalar(nm[:, b, :], mx[:, b, :], -SCALE, None, ALU.mult).then_inc(neg_done, 1)

                    def softmax_out(h, p_):
                        N = NP * h + p_
                        b = p_ % 2
                        dve.wait_ge(exp_done, 2 * N + 2)
                        dve.reciprocal(rl[:, b, :], l[:, b, :]).then_inc(rl_done, 1)
                        dve.wait_ge(rl_done, N + 1)
                        for t in range(2):
                            dve.tensor_scalar(p[b][:, t, :], p[b][:, t, :], rl[:, b, t:t + 1], None, ALU.mult)\
                                .then_inc(p_ready, 1)

                    def finish(h, s):
                        dve.wait_ge(pv_done, NS * h + s + 1)
                        if s == 0:
                            for b in range(NS):
                                dve.wait_ge(z_free[b], C0 + MEM_C * h + G + 1)
                        tok = slice(s * SEQ, (s + 1) * SEQ)
                        out, o, g = y[:, tok], o_ps[:], gate[:, tok]
                        if i == 0:
                            out = out.rearrange("p (i r) -> p r i", r=RES)
                            o, g = (a.rearrange("p (r i) -> p r i", r=RES) for a in (o, g))
                        dve.tensor_tensor(out, o, g, ALU.mult).then_inc(y_done, 1)

                    def rest(h, n):
                        if n == 0:
                            softmax_in(h, 2)
                            softmax_out(h, 2)
                            softmax_in(h, 3)
                            softmax_out(h, 3)
                        if n == 2:
                            finish(h, 0)
                        if n == 4:
                            finish(h, 1)

                    def memory_rows(b):
                        dve.wait_ge(mh_in[b], 16)
                        for k in range(b * KC // 2, (b + 1) * KC // 2):
                            need(dve, ml_done, k - 1)
                            dve.tensor_scalar(m_g[k % 2][:], m_hat[:, k, :], gains[:, 2 * i + 1, k:k + 1], None, ALU.mult)\
                                .then_inc(mg_done, 1)
                            dve.wait_ge(mh_done, k + 1)
                            dve.tensor_tensor(m_lo[:, k, :], m_g[k % 2][:], m_hi[:, k, :].bitcast(F32), ALU.subtract)\
                                .then_inc(ml_done, 1)

                    def head(h, before, last):
                        for n in range(2 * MEM_C):
                            c = n // 2
                            if n % 2 == 0:
                                split_lo(dve, C0 + MEM_C * h + c + 1, (C0 + c + 1) % 2,
                                         nk=FC if last and c == MEM_C - 1 else KC)
                            if before is not None:
                                rest(before, n)
                            if n == 7:
                                dve.wait_ge(vtr_done, h + 1)
                                need(dve, pv_done, NS * h)
                                dve.tensor_copy(v[:], v_ps[:].rearrange("p (t e) -> p t e", e=HD)).then_inc(v_ready, 1)
                            if before is None and n < 2:
                                memory_rows(n)
                            if n == 5:
                                for p_ in (0, 1):
                                    softmax_in(h, p_)
                                for p_ in (0, 1):
                                    softmax_out(h, p_)
                            if n == 2 * G:
                                need(dve, y_stored, 16 * h)
                    head(0, None, False)
                    with dve.Fori(1, MEM_HEADS - 1) as h:
                        head(h, h - 1, False)
                    head(MEM_HEADS - 1, MEM_HEADS - 2, True)
                    for n in range(5):
                        rest(MEM_HEADS - 1, n)

        def output_projection(i, xT, acc, y_a, y_b, st):
            tag = "ab"[i]
            y_parts = [y_a[:, f, :] for f in range(2 * KC)] + [y_b[:, f, :] for f in range(2 * FC - 2 * KC)]
            y_hi, y_lo = y_parts[:FC], y_parts[FC:]
            NB = 3
            y_raw = [sb(f"{tag}y_raw{b}", [P, TOK], stack=st) for b in range(NB)]
            res = sb(tag + "res", [P, 2, TOK], stack=st)
            y_in = [sem(f"{tag}y_in{b}") for b in range(NB)]
            yh, yl, res_in = (sem(f"{tag}out_" + n) for n in ("yh", "yl", "res_in"))
            res_in2 = sem(f"{tag}out_res_in2")
            sq_done, acc_done = sem(f"{tag}out_sq_done"), sem(f"{tag}out_acc_done")
            w = A[tag + "_wout"][0]
            C0 = C_OUT[i]
            last_stage = i == 1
            PAIRS = KC // 2
            TAIL = FC - 2
            block = st.enter_context(nc.Block())
            rin = (res_in, res_in2)
            first_banks = [[z_ps[s][:] for s in range(NS)], [s_ps[:, s * SEQ:(s + 1) * SEQ] for s in range(NS)]]

            @block.sync
            def _(sp):
                for f in range(FC):
                    need(sp, yl, f + 1 - NB)
                    sp.dma_start(y_raw[f % NB][:], y_scratch[i][f]).then_inc(y_in[f % NB], 16)

                def pair(d2):
                    for b in range(2):
                        w_load(sp, w, (2 * d2 + b) * P, (C0 + b) % 2, C0 + 2 * d2 + b, nk=FC)
                with sp.Fori(1, PAIRS) as d2:
                    pair(d2)
                if not last_stage:
                    w_load(sp, A["b_win"][0], GLR, C_LR % 2, C_LR)
                    for s in range(NS):
                        sp.wait_ge(z_free[s], C0 + KC)
                    sp.dma_start(xt_scratch, xT[:]).then_inc(x_stored, 16)

            @block.gpsimd
            def _(pool):
                def load(c, b):
                    if not isinstance(c, int) or c >= 2:
                        for s in range(NS):
                            pool.wait_ge(z_free[s], C0 + c - 1)
                    pool.dma_start(res[:, b, :], xt_scratch[:, c, :]).then_inc(rin[b], 16)

                def add(c, b):
                    pool.wait_ge(sq_done, c + 1)
                    need(pool, acc_done, c - 1)
                    pool.tensor_tensor(acc[:], acc[:], y_raw[b][:], ALU.add).then_inc(acc_done, 1)
                load(0, 0)
                load(1, 1)
                add(1, 1)
                with pool.Fori(1, PAIRS) as d2:
                    for b in range(2):
                        load(2 * d2 + b, b)
                        add(2 * d2 + b, b)

            @block.tensor
            def _(pe):
                def pair(d2):
                    for n in range(4):
                        unit(pe, C0 + 2 * d2 + n // 2, (C0 + n // 2) % 2, n % 2, y_hi, y_lo, nk=FC)

                def step(b, f):
                    pe.wait_ge(lo_done, C0 + b + 1)
                    pe.wait_ge(yl, f + 1)
                    for s in range(NS):
                        out, tok = first_banks[b][s], slice(s * SEQ, (s + 1) * SEQ)
                        pe.matmul(out, w_hi[(C0 + b) % 2][:, f, :], y_hi[f][:, tok], start=(f == 0), stop=False)
                        pe.matmul(out, w_hi[(C0 + b) % 2][:, f, :], y_lo[f][:, tok], start=False, stop=False)
                        mm = pe.matmul(out, w_lo[(C0 + b) % 2][:, f, :], y_hi[f][:, tok], start=False, stop=(f == FC - 1))
                        if f == FC - 1:
                            mm.then_inc(z_ready[s], 1)
                for s in range(NS):
                    pe.wait_ge(z_free[s], C0)
                for f in range(TAIL):
                    for b in range(2):
                        step(b, f)
                for b in range(2):
                    for f in range(TAIL, FC):
                        step(b, f)
                with pe.Fori(1, PAIRS) as d2:
                    pair(d2)

            @block.scalar
            def _(act):
                split_hi(act, C0 + 1, halves(C0, 2, 0, 1), (C0 + 1) % 2, nk=FC)
                for f in range(FC):
                    act.wait_ge(y_in[f % NB], 16 * (f // NB) + 16)
                    act.activation(y_hi[f], y_raw[f % NB][:], ACT.Copy).then_inc(yh, 1)

                def square(c, b):
                    for s in range(NS):
                        act.wait_ge(z_free[s], C0 + c + 1)
                    if isinstance(c, int) and c < 2:
                        act.wait_ge(yl, FC)
                    else:
                        act.wait_ge(acc_done, c - 1)
                    out = acc if isinstance(c, int) and c == 0 else y_raw[b]
                    act.activation(out[:], xT[:, c, :] if isinstance(c, int) else xT[:, bass.ds(c, 1), :].rearrange(
                        "p o t -> p (o t)"), ACT.Square).then_inc(sq_done, 1)

                def pair(d2, end):
                    for b in range(2):
                        if not (end and b == 1):
                            split_hi(act, C0 + 2 * d2 + b + 1, halves(C0, 2, d2, b + 1), (C0 + b + 1) % 2, nk=FC)
                        square(2 * d2 + b, b)
                split_hi(act, C0 + 2, halves(C0, 2, 0, 2), C0 % 2, nk=FC)
                square(0, 0)
                square(1, 1)
                with act.Fori(1, PAIRS - 1) as d2:
                    pair(d2, False)
                pair(PAIRS - 1, True)

            @block.vector
            def _(dve):
                split_lo(dve, C0 + 1, (C0 + 1) % 2, nk=FC)
                for f in range(FC):
                    dve.wait_ge(yh, f + 1)
                    dve.tensor_tensor(y_lo[f], y_raw[f % NB][:], y_hi[f].bitcast(F32), ALU.subtract).then_inc(yl, 1)

                def pair(d2, end, first=False):
                    if first:
                        split_lo(dve, C0 + 2, C0 % 2, nk=FC)
                    for n in range(4):
                        b, s = n // 2, n % 2
                        if s == 0 and not first and not (end and b == 1):
                            split_lo(dve, C0 + 2 * d2 + b + 1, (C0 + b + 1) % 2, nk=FC)
                        dve.wait_ge(rin[b], 16 * d2 + 16)
                        dve.wait_ge(z_ready[s], C0 + 2 * d2 + b + 1)
                        dve.tensor_tensor(xT[:, 2 * d2 + b, s * SEQ:(s + 1) * SEQ],
                                          first_banks[b][s] if first else z_ps[s][:],
                                          res[:, b, s * SEQ:(s + 1) * SEQ], ALU.add).then_inc(z_free[s], 1)
                pair(0, False, first=True)
                with dve.Fori(1, PAIRS - 1) as d2:
                    pair(d2, False)
                pair(PAIRS - 1, True)

        gla = make_gla(nc, A, locals())

        with ExitStack() as layer:
            hi = sb("ah_hi", [P, KC, TOK], F32R, stack=layer)
            lo = sb("ah_lo", [P, KC, TOK], F32R, stack=layer)
            with ExitStack() as st:
                xa = sb("xa", [P, KC, TOK], stack=st)
                acc = sb("x_acc", [P, TOK], stack=st)
                mt0 = sb("mt0", [P, KC, MT], stack=st)
                with ExitStack() as inner:
                    load_and_transpose(xa, mt0, inner)
                norm_split("an", xa, acc, False, 0, hi, lo, True, C_DIL, (A["a_win"][0], DIL_W), 2, st)
            dilated(hi, lo)
            memory(0, hi, lo)
        with ExitStack() as layer:
            h_parts = sb("b_parts", [P, 2 * KC, TOK], F32R, stack=layer)
            hi, lo = h_parts[:, 0:KC, :], h_parts[:, KC:2 * KC, :]
            with ExitStack() as inner:
                xb = sb("xb", [P, KC, TOK], stack=inner)
                acc = sb("xb_acc", [P, TOK], stack=inner)
                with ExitStack() as st:
                    y_b = sb("ay_b", [P, 2 * FC - 2 * KC, TOK], F32R, stack=st)
                    output_projection(0, xb, acc, h_parts, y_b, st)
                with ExitStack() as st:
                    norm_split("bn", xb, acc, True, 2, hi, lo, False, C_LR, (A["b_win"][0], GQ), 3, st)
            gla(hi, lo)
            memory(1, hi, lo)
        with ExitStack() as layer:
            xb = sb("xc", [P, KC, TOK], stack=layer)
            acc = sb("xc_acc", [P, TOK], stack=layer)
            with ExitStack() as st:
                y_a = sb("by_a", [P, 2 * KC, TOK], F32R, stack=st)
                y_b = sb("by_b", [P, 2 * FC - 2 * KC, TOK], F32R, stack=st)
                output_projection(1, xb, acc, y_a, y_b, st)
            final_norm(nc, A, xb, acc, sb, sem, ident, ones, s_ps, t_ps, o_ps, z_ps, sum_done, var_done, root,
                       step)


def final_norm(nc, A, xT, acc, sb, sem, ident, ones, s_ps, t_ps, o_ps, z_ps, sum_done, var_done, root, step):
    with ExitStack() as st:
        gain = sb("f_gain", [P, D], stack=st)
        grow = sb("f_grow", [1, D], stack=st)
        rstd, var, tmp = (sb("f_" + n, [P, NT], stack=st) for n in ("rstd", "var", "tmp"))
        rows = [sb(f"f_rows{i}", [P, D], stack=st) for i in range(3)]
        g_in, g_done, g_moved, turned, moved = (sem("f_" + n) for n in ("g_in", "g_done", "g_moved", "turned", "moved"))
        M0 = 5
        stored = [sem(f"f_stored{i}") for i in range(3)]
        block = st.enter_context(nc.Block())
        turn_ps = (s_ps, t_ps)

        @block.scalar
        def _(act):
            act.preload_act_table_set("natural_log_exp_and_others")
            root_start(act, rstd[:], var[:], var_done, root, M0)
            for b in range(2):
                act.wait_ge(g_done, b + 1)
                act.activation(gain[:, b * 512:(b + 1) * 512], z_ps[b][:], ACT.Copy).then_inc(g_moved, 1)

        @block.tensor
        def _(pe):
            for t in range(NT):
                mm = pe.matmul(o_ps[:, t:t + 1], acc[:, t * P:(t + 1) * P], ones[:, 0:1], start=True, stop=True)
            mm.then_inc(sum_done, 1)
            pe.wait_ge(g_in, 16)
            for b in range(2):
                pe.matmul(z_ps[b][:], ones[0:1, :], grow[:, b * 512:(b + 1) * 512], start=True, stop=True)\
                    .then_inc(g_done, 1)
            for t in range(NT):
                need(pe, moved, t - 1)
                for k in range(KC):
                    tr = pe.transpose(turn_ps[t % 2][:, k * P:(k + 1) * P], xT[:, k, t * P:(t + 1) * P], ident[:])
                tr.then_inc(turned, 1)

        @block.vector
        def _(dve):
            dve.wait_ge(sum_done, M0)
            dve.tensor_scalar(var[:], o_ps[:, 0:NT], 1.0 / D, EPS, ALU.mult, ALU.add).then_inc(var_done, 1)
            root_refine(dve, rstd[:], var[:], tmp[:], root, step, M0)
            dve.wait_ge(step, 4 * (M0 + 1))
            dve.wait_ge(g_moved, 2)
            for t in range(NT):
                dve.wait_ge(turned, t + 1)
                need(dve, stored[t % 3], 16 * (t // 3))
                dve.scalar_tensor_tensor(out=rows[t % 3][:], in0=turn_ps[t % 2][:], scalar=rstd[:, t:t + 1],
                                         in1=gain[:], op0=ALU.mult, op1=ALU.mult).then_inc(moved, 1)

        @block.sync
        def _(sp):
            sp.dma_start(grow[:], A["lnf"].rearrange("(o d) -> o d", o=1)).then_inc(g_in, 16)
            for t in range(NT):
                out = A["y_prompt" if t < SEQ // P else "y_sample"][0]
                i = t % (SEQ // P)
                sp.wait_ge(moved, t + 1)
                sp.dma_start(out[i * P:(i + 1) * P, :], rows[t % 3][:]).then_inc(stored[t % 3], 16)
            for b in range(3):
                sp.wait_ge(stored[b], 16 * len(range(b, NT, 3)))


def make_gla(nc, A, env):
    sb, sem, unit, w_load = env["sb"], env["sem"], env["unit"], env["w_load"]
    split_hi, split_lo, silu_pair = env["split_hi"], env["split_lo"], env["silu_pair"]
    z_ps, s_ps, t_ps, o_ps, v_ps = env["z_ps"], env["s_ps"], env["t_ps"], env["o_ps"], env["v_ps"]
    z_ready, z_free, ident, ones = env["z_ready"], env["z_free"], env["ident"], env["ones"]
    carrier = env["carrier"]
    w_raw, onorm, eps_col, y_scratch = env["w_raw"], env["onorm"], env["eps_col"], env["y_scratch"]

    NL = len(LEVELS)
    NE = NL + 1
    NLD = NL + 2
    TPS = SEQ // P
    QS = float(GDK) ** -0.5
    Q, K, V, G = 0, 1, 2, 4
    SLOTS = 2 * GLA_C
    FW, BW = 0, 1
    ST = TPS - 1

    def stage(hi, lo):
        with ExitStack() as st:
            def buf(name, shape):
                return sb("g_" + name, shape, stack=st)

            q, k = buf("q", [P, TOK]), buf("k", [P, TOK])
            vT = buf("vT", [P, TOK])
            v = buf("v", [P, NT, GDV])
            gate = buf("gate", [P, 2, TOK])
            b = [buf("b_f", [P, TOK]), buf("b_b", [P, TOK])]
            E = [buf("E0", [P, 2, TOK]), buf("E1", [P, 2, TOK])]
            att = buf("att", [P, NT, P])
            masks = sb("g_masks", [P, NL + 1, P], U32, stack=st)
            qi = buf("qi", [P, 2, TOK])
            kd = buf("kd", [P, 2, NT, P])
            out_sb = kd[:].rearrange("p s t e -> p s (t e)").rearrange("p s (f i) -> p s f i", f=2)
            S = buf("S", [P, 2, NS, ST, GDV])
            rstd = buf("rstd", [P, SEQ])
            lrT = sb("g_lrT", [2 * RANK, TOK], stack=st)
            wg = sb("g_wg", [2 * RANK, 2, GDK], stack=st)
            bg, bgh = buf("bg", [P, 2, GLA_HEADS]), buf("bgh", [P, 2])
            starts = buf("starts", [P, SEQ])
            dcol, dec = buf("dcol", [P, 2, NT]), buf("dec", [P, 2, NT])
            sq = [w_raw[i][:, KC:FC, :].rearrange("p k c -> p (k c)") for i in range(2)]

            e0 = E[0][:].rearrange("p a t -> p (a t)")
            e1 = E[1][:].rearrange("p a t -> p (a t)")
            SH = 4
            g = [e0[:, 0:TOK], e1[:, SH:SH + TOK]]
            L = [e0[:, TOK + s * SEQ:TOK + (s + 1) * SEQ] for s in range(NS)]

            (bgh_done, bg_in, c_in, wg_zero, wg_in, x_done, min_done, abs_done, ex_done, ln_done, g_done, scan_done, dcol_done,
             dec_done, sub_done, e_done, op_done, qsub_done, qe_done, qi_done, zero_done, lev_done, mask_done, kd_ready,
             opk_done, st_mm, st_done, vtr_done, v_ready, out_done, out_moved, sq_done, ssq_done, sd_done, rln_done, t_done, y_done,
             y_stored) = (sem("gla_" + n) for n in (
                 "bgh_done", "bg_in", "c_in", "wg_zero", "wg_in", "x_done", "min_done", "abs_done", "ex_done", "ln_done",
                 "g_done", "scan_done", "dcol_done", "dec_done", "sub_done", "e_done", "op_done", "qsub_done",
                 "qe_done", "qi_done", "zero_done", "lev_done", "mask_done", "kd_ready", "opk_done", "st_mm", "st_done",
                 "vtr_done", "v_ready", "out_done", "out_moved", "sq_done", "ssq_done", "sd_done", "rln_done",
                 "t_done", "y_done", "y_stored"))
            w = A["b_win"][0]
            block = st.enter_context(nc.Block())

            def toks(s):
                return slice(s * SEQ, (s + 1) * SEQ)

            def chunk(h, c):
                return C_GLA + GLA_C * h + c

            def slot_of(c):
                return (C_GLA + c) % 2

            def entries(n):
                return [e for e in range(NE) if n == (e + 3 if e < 2 else e + 4)]

            @block.sync
            def _(sp):
                sp.dma_start(masks[:], A["c_masks"]).then_inc(c_in, 16)
                sp.dma_start(starts[:], A["c_starts"][:, 0:SEQ]).then_inc(c_in, 16)

                def head(h, start=0):
                    cols = [GQ + h * GDK, GK + h * GDK, GV + h * GDV, GV + h * GDV + P, GATE_B + h * GDV,
                            GATE_B + h * GDV + P]
                    for c in range(start, GLA_C):
                        w_load(sp, w, cols[c], slot_of(c), chunk(h, c))
                head(0, start=1)
                with sp.Fori(1, GLA_HEADS) as h:
                    head(h)
                w_load(sp, w, GQM, C_MEM[1] % 2, C_MEM[1])

            @block.gpsimd
            def _(pool):
                pool.memset(wg[:], 0.0).then_inc(wg_zero, 1)
                for d, n in enumerate(("b_bg_f", "b_bg_b")):
                    pool.dma_start(bg[:, d, :], A[n][0].rearrange("(h p) -> p h", p=P)).then_inc(bg_in, 16)
                pool.wait_ge(wg_zero, 1)

                def load_gates(col):
                    for d, n in enumerate(("b_wg_f", "b_wg_b")):
                        pool.dma_start(wg[d * RANK:(d + 1) * RANK, d, :], A[n][0][:, bass.ds(col, GDK)])\
                            .then_inc(wg_in, 16)

                def operands(h, n):
                    pool.wait_ge(e_done, NE * h + n + 1)
                    if n == 0:
                        for s in range(NS):
                            pool.wait_ge(z_free[s], chunk(h, K) + 1)
                    a = q if n < NL else k
                    pool.tensor_tensor(E[n % 2][:, 0, :], E[n % 2][:, 0, :], a[:], ALU.mult).then_inc(op_done, 1)

                def squares(h, s):
                    pool.wait_ge(out_moved, 4 * h + 2 * s + 2)
                    if s == 1:
                        pool.wait_ge(ssq_done, 2 * h + 1)
                    for f in range(2):
                        pool.tensor_tensor(sq[f], out_sb[:, s, f, :], out_sb[:, s, f, :], ALU.mult).then_inc(sq_done, 1)

                def rest(h, n):
                    if n == 4:
                        squares(h, 0)
                    if n == 5:
                        squares(h, 1)
                    if n == 7:
                        pool.wait_ge(y_done, 4 * h + 4)
                        for f in range(2):
                            pool.dma_start(y_scratch[1][2 * h + f], gate[:, f, :]).then_inc(y_stored, 16)

                def head(h, before, col_next):
                    for n in range(SLOTS):
                        if before is not None:
                            rest(before, n)
                        if n == 4:
                            pool.wait_ge(x_done, 2 * h + 2)
                            load_gates(col_next)
                        for e in entries(n):
                            operands(h, e)
                        if n == 9:
                            need(pool, ssq_done, 2 * h)

                load_gates(0)
                head(0, None, GDK)
                with pool.Fori(1, GLA_HEADS - 1) as h:
                    head(h, h - 1, (h + 1) * GDK)
                head(GLA_HEADS - 1, GLA_HEADS - 2, 0)
                for n in range(8):
                    rest(GLA_HEADS - 1, n)
                pool.wait_ge(y_stored, 32 * GLA_HEADS)
                pool.wait_ge(wg_in, 32 * (GLA_HEADS + 1))

            @block.tensor
            def _(pe):
                def gates(h):
                    pe.wait_ge(wg_in, 32 * h + 32)
                    need(pe, kd_ready, 2 * h)
                    for d, dst in enumerate((s_ps, t_ps)):
                        for s in range(NS):
                            mm = pe.matmul(dst[:, toks(s)], wg[:, d, :], lrT[:, toks(s)], start=True, stop=True)
                        mm.then_inc(x_done, 1)

                def level(h, i):
                    dst = (s_ps, t_ps)[i % 2]
                    if i == 0:
                        for s in range(NS):
                            pe.wait_ge(z_free[s], chunk(h, K) + 1)
                        a, c = k, q
                    else:
                        pe.wait_ge(op_done, NE * h + i)
                        if i < NL:
                            pe.wait_ge(opk_done, (NE - 1) * h + i)
                        a, c = E[(i - 1) % 2][:, 1, :] if i < NL else k, E[(i - 1) % 2][:, 0, :]
                    if i < 2:
                        pe.wait_ge(abs_done, 4 * h + 2 * i + 2)
                    else:
                        pe.wait_ge(mask_done, (NL + 1) * h + i - 1)
                    for t in range(NT):
                        tok = slice(t * P, (t + 1) * P)
                        mm = pe.matmul(dst[:, tok], a[:, tok], c[:, tok], start=True, stop=True)
                    mm.then_inc(lev_done, 1)

                def turn_keys(h):
                    pe.wait_ge(op_done, NE * h + NE)
                    pe.wait_ge(opk_done, (NE - 1) * (h + 1))
                    for d, dst in enumerate((s_ps, t_ps)):
                        pe.wait_ge(mask_done, (NL + 1) * h + NL + d)
                        for t in range(NT):
                            tr = pe.transpose(dst[:, t * P:(t + 1) * P], E[NL % 2][:, d, t * P:(t + 1) * P], ident[:])
                    tr.then_inc(lev_done, 1)

                def turn_values(h, m):
                    f, s = m // 2, m % 2
                    pe.wait_ge(z_free[s], chunk(h, V + f) + 1)
                    need(pe, v_ready, 4 * h + m)
                    if m == 0:
                        need(pe, out_moved, 4 * h)
                    for i in range(TPS):
                        t = s * TPS + i
                        tr = pe.transpose(v_ps[:, i * P:(i + 1) * P], vT[:, t * P:(t + 1) * P], ident[:])
                    tr.then_inc(vtr_done, 1)

                def states(h, r):
                    s, i = r // ST, r % ST
                    dst = (o_ps, v_ps)[r % 2]
                    if r == 0:
                        pe.wait_ge(kd_ready, 2 * h + 2)
                        pe.wait_ge(v_ready, 4 * h + 4)
                    if r >= 2:
                        pe.wait_ge(st_done, 2 * ST * h + r - 1)
                    for d in range(2):
                        t = s * TPS + (i if d == FW else TPS - 1 - i)
                        mm = pe.matmul(dst[:, d * GDV:(d + 1) * GDV], kd[:, d, t, :], v[:, t, :], start=True, stop=True)
                    mm.then_inc(st_mm, 1)

                def outputs(h, s):
                    for f, dst in enumerate((o_ps, v_ps)):
                        if s == 0 and f == 0:
                            pe.wait_ge(st_done, 2 * ST * (h + 1))
                            pe.wait_ge(qi_done, h + 1)
                        if s == 1:
                            pe.wait_ge(out_moved, 4 * h + 2)
                        cols = slice(f * P, (f + 1) * P)
                        for i in range(TPS):
                            t = s * TPS + i
                            tok = slice(t * P, (t + 1) * P)
                            dt = dst[:, i * P:(i + 1) * P]
                            mm = pe.matmul(dt, v[:, t, cols], att[:, t, :], start=(i == 0), stop=False,
                                           skip_group_check=True)
                            if i > 0:
                                mm = pe.matmul(dt, S[:, FW, s, i - 1, cols], qi[:, 0, tok], start=False,
                                               stop=(i == TPS - 1), skip_group_check=True)
                            if i < TPS - 1:
                                mm = pe.matmul(dt, S[:, BW, s, TPS - 2 - i, cols], qi[:, 1, tok], start=False,
                                               stop=False, skip_group_check=True)
                        mm.then_inc(out_done, 1)

                def sum_squares(h, s):
                    pe.wait_ge(sq_done, 4 * h + 2 * s + 2)
                    if s == 0:
                        pe.wait_ge(out_moved, 4 * h + 4)
                    else:
                        pe.wait_ge(sd_done, 2 * h + 1)
                    pe.matmul(o_ps[:], ones[:], sq[0], start=True, stop=False)
                    pe.matmul(o_ps[:], ones[:], sq[1], start=False, stop=True).then_inc(ssq_done, 1)

                def rest(h, n):
                    if n == 0:
                        level(h, NL)
                        turn_keys(h)
                    if n in (1, 2):
                        for r in (2 * n - 2, 2 * n - 1):
                            states(h, r)
                    if n == 3:
                        outputs(h, 0)
                    if n == 4:
                        outputs(h, 1)
                    if n in (5, 6):
                        sum_squares(h, n - 5)

                def head(h, before):
                    for n in range(SLOTS):
                        c = n // 2
                        if before is not None and n == 3:
                            states(before, 4)
                            states(before, 5)
                        unit(pe, chunk(h, c), slot_of(c), n % 2, hi, lo)
                        if before is not None:
                            rest(before, n)
                        if n == 1:
                            gates(h)
                        if n == 9:
                            need(pe, st_done, 2 * ST * h)
                            need(pe, sd_done, 2 * h)
                        if 5 <= n < 9:
                            turn_values(h, n - 5)
                        if n >= 5:
                            level(h, n - 5)
                for s in range(NS):
                    pe.wait_ge(z_free[s], C_LR + 1)
                head(0, None)
                with pe.Fori(1, GLA_HEADS) as h:
                    head(h, h - 1)
                for n in range(7):
                    if n == 3:
                        states(GLA_HEADS - 1, 4)
                        states(GLA_HEADS - 1, 5)
                    rest(GLA_HEADS - 1, n)

            @block.scalar
            def _(act):
                def log_gates(h, d):
                    src = (s_ps, t_ps)[d]
                    act.wait_ge(min_done, 2 * h + d + 1)
                    for s in range(NS):
                        n = 4 * h + 2 * d + s
                        if d == 1:
                            act.wait_ge(g_done, 4 * h + s + 1)
                        act.activation(L[s], src[:, toks(s)], ACT.Abs, bias=bgh[:, d:d + 1]).then_inc(abs_done, 1)
                        act.wait_ge(abs_done, n + 1)
                        act.activation(L[s], L[s], ACT.Exp, scale=-1.0).then_inc(ex_done, 1)
                        act.wait_ge(ex_done, n + 1)
                        act.activation(L[s], L[s], ACT.Ln, bias=1.0).then_inc(ln_done, 1)

                def decays(h):
                    act.wait_ge(dcol_done, 2 * h + 2)
                    need(act, st_done, 2 * ST * h)
                    act.activation(dec[:], dcol[:], ACT.Exp, scale=1.0 / TAU).then_inc(dec_done, 1)

                def exps(h, n):
                    act.wait_ge(sub_done, NE * h + n + 1)
                    if n == NL - 1:
                        act.activation(E[n % 2][:, 0, :], E[n % 2][:, 0, :], ACT.Exp, scale=1.0 / TAU).then_inc(e_done, 1)
                    elif n < NL:
                        act.activation(E[n % 2][:], E[n % 2][:], ACT.Exp, scale=1.0 / TAU).then_inc(e_done, 1)
                    else:
                        act.activation(E[n % 2][:, 1, :], b[BW][:], ACT.Exp, scale=1.0 / TAU)
                        act.activation(E[n % 2][:, 0, :], E[n % 2][:, 0, :], ACT.Exp, scale=1.0 / TAU).then_inc(e_done, 1)

                def query_exps(h):
                    act.wait_ge(qsub_done, h + 1)
                    act.activation(qi[:, 0, :], b[FW][:], ACT.Exp, scale=1.0 / TAU)
                    act.activation(qi[:, 1, :], qi[:, 1, :], ACT.Exp, scale=1.0 / TAU).then_inc(qe_done, 1)

                def move_keys(h):
                    act.wait_ge(lev_done, NLD * (h + 1))
                    for d, src in enumerate((s_ps, t_ps)):
                        act.activation(kd[:, d, :, :], src[:].rearrange("p (t e) -> p t e", e=P), ACT.Copy)\
                            .then_inc(kd_ready, 1)

                def move_outputs(h, s):
                    for f, src in enumerate((o_ps, v_ps)):
                        act.wait_ge(out_done, 4 * h + 2 * s + f + 1)
                        act.activation(out_sb[:, s, f, :], src[:], ACT.Copy).then_inc(out_moved, 1)

                def root(h, s):
                    act.wait_ge(ssq_done, 2 * h + s + 1)
                    if s == 1:
                        act.wait_ge(t_done, 4 * h + 2)
                    act.activation(rstd[:], o_ps[:], ACT.Ln, bias=eps_col[:], scale=1.0 / GDV).then_inc(rln_done, 1)
                    act.wait_ge(rln_done, 2 * h + s + 1)
                    act.activation(rstd[:], rstd[:], ACT.Exp, scale=-0.5).then_inc(sd_done, 1)

                def rest(h, n):
                    if n == 1:
                        move_keys(h)
                    if n in (4, 5):
                        move_outputs(h, n - 4)
                    if n in (6, 7):
                        root(h, n - 6)

                def move(h, n):
                    c, s = n // 2, n % 2
                    j = chunk(h, c)
                    if c >= G:
                        if s == 1:
                            if c == G:
                                need(act, y_stored, 32 * h)
                            silu_pair(act, j, [gate[:, c - G, toks(b_)] for b_ in range(NS)])
                        return
                    act.wait_ge(z_ready[s], j + 1)
                    if n == 0:
                        need(act, op_done, NE * h)
                    if c == V or c == V + 1:
                        need(act, vtr_done, 4 * h + 2 * (c - V) + s - 1)
                    if c == Q:
                        act.activation(q[:, toks(s)], z_ps[s][:], ACT.Copy, scale=QS).then_inc(z_free[s], 1)
                    else:
                        act.activation((k if c == K else vT)[:, toks(s)], z_ps[s][:], ACT.Copy).then_inc(z_free[s], 1)

                def head(h, before):
                    for n in range(SLOTS):
                        if n % 2 == 0:
                            split_hi(act, chunk(h, n // 2) + 1, halves(C_GLA, GLA_C, h, n // 2 + 1), slot_of(n // 2 + 1))
                        if before is not None:
                            rest(before, n)
                        if n == 2:
                            act.preload_act_table_set("natural_log_exp_and_others")
                            log_gates(h, FW)
                        move(h, n)
                        if n == 2:
                            log_gates(h, BW)
                        for e in entries(n):
                            exps(h, e)
                        if n == 4:
                            decays(h)
                        if n == 9:
                            query_exps(h)
                            need(act, y_done, 4 * h)
                split_hi(act, C_GLA, C_GLA // 2, C_GLA % 2)
                act.wait_ge(bg_in, 16 * 2)
                for s in range(NS):
                    act.wait_ge(z_ready[s], C_LR + 1)
                    act.activation(lrT[:, toks(s)], z_ps[s][0:2 * RANK, :], ACT.Copy).then_inc(z_free[s], 1)
                head(0, None)
                with act.Fori(1, GLA_HEADS) as h:
                    head(h, h - 1)
                for n in range(8):
                    rest(GLA_HEADS - 1, n)

            @block.vector
            def _(dve):
                def minima(h, d):
                    src = (s_ps, t_ps)[d]
                    dve.wait_ge(x_done, 2 * h + d + 1)
                    need(dve, lev_done, NLD * h)
                    dve.tensor_scalar(g[d], src[:], bgh[:, d:d + 1], 0.0, ALU.add, ALU.min).then_inc(min_done, 1)

                def log_sums(h, d):
                    for s in range(NS):
                        n = 4 * h + 2 * d + s
                        dve.wait_ge(ln_done, n + 1)
                        dve.tensor_tensor(g[d][:, toks(s)], g[d][:, toks(s)], L[s], ALU.subtract).then_inc(g_done, 1)
                        dve.wait_ge(g_done, n + 1)
                        if d == FW:
                            dve.tensor_tensor_scan(b[FW][:, toks(s)], starts[:], g[FW][:, toks(s)], 0.0, ALU.mult,
                                                   ALU.add).then_inc(scan_done, 1)
                        else:
                            dve.tensor_tensor_scan(b[BW][:, toks(s)], e1[:, SH - 1 + s * SEQ:SH - 1 + (s + 1) * SEQ],
                                                   starts[:], 0.0, ALU.add, ALU.mult).then_inc(scan_done, 1)

                def tile_sums(h):
                    dve.wait_ge(scan_done, 4 * h + 4)
                    need(dve, dec_done, h)
                    last = [x.rearrange("p (t i) -> p t i", i=P)[:, :, P - 1] for x in (b[FW][:], b[BW][:], g[BW])]
                    dve.tensor_copy(dcol[:, FW, :], last[0]).then_inc(dcol_done, 1)
                    dve.tensor_tensor(dcol[:, BW, :], last[1], last[2], ALU.add).then_inc(dcol_done, 1)

                def exponents(h, n):
                    if n == 0:
                        dve.wait_ge(dcol_done, 2 * h + 2)
                    if n >= 2:
                        dve.wait_ge(lev_done, NLD * h + n)
                    if n == NL:
                        bf = b[FW][:].rearrange("p (t i) -> p t i", i=P)
                        dve.tensor_tensor(E[n % 2][:, 0, :].rearrange("p (t i) -> p t i", i=P),
                                          dcol[:, FW, :].rearrange("p (t o) -> p t o", o=1).to_broadcast([P, NT, P]), bf,
                                          ALU.subtract).then_inc(sub_done, 1)
                        return
                    m = LEVELS[n]
                    nb = TOK // (2 * m)

                    def view(a):
                        return a.rearrange("p (n u m) -> p n u m", u=2, m=m)
                    bf, bb = view(b[FW][:]), view(b[BW][:])
                    eq, ek = view(E[n % 2][:, 0, :]), view(E[n % 2][:, 1, :])
                    mid_f = bf[:, :, 0, m - 1:m].to_broadcast([P, nb, m])
                    mid_b = bb[:, :, 1, 0:1].to_broadcast([P, nb, m])
                    dve.tensor_tensor(eq[:, :, 1, :], bf[:, :, 1, :], mid_f, ALU.subtract)
                    last = dve.tensor_tensor(eq[:, :, 0, :], mid_b, bb[:, :, 0, :], ALU.subtract)
                    if m == 1:
                        last.then_inc(sub_done, 1)
                        return
                    dve.tensor_tensor(ek[:, :, 0, :], mid_f, bf[:, :, 0, :], ALU.subtract)
                    dve.tensor_tensor(ek[:, :, 1, :], bb[:, :, 1, :], mid_b, ALU.subtract).then_inc(sub_done, 1)

                def key_operands(h, n):
                    if n == NL - 1:
                        return
                    dve.wait_ge(e_done, NE * h + n + 1)
                    dve.tensor_tensor(E[n % 2][:, 1, :], E[n % 2][:, 1, :], k[:], ALU.mult).then_inc(opk_done, 1)

                def query_decays(h):
                    dve.wait_ge(qe_done, h + 1)
                    dve.tensor_tensor(qi[:, 0, :], qi[:, 0, :], q[:], ALU.mult)
                    dve.tensor_tensor(qi[:, 1, :], qi[:, 1, :], q[:], ALU.mult).then_inc(qi_done, 1)

                def query_exponents(h):
                    need(dve, out_done, 4 * h)
                    dve.tensor_tensor(qi[:, 1, :].rearrange("p (t i) -> p t i", i=P),
                                      dcol[:, BW, :].rearrange("p (t o) -> p t o", o=1).to_broadcast([P, NT, P]),
                                      b[BW][:].rearrange("p (t i) -> p t i", i=P), ALU.subtract).then_inc(qsub_done, 1)

                def pick(h, i):
                    dve.wait_ge(lev_done, NLD * h + i + 1)
                    if i == 0:
                        need(dve, out_done, 4 * h)
                        dve.memset(att[:], 0.0).then_inc(zero_done, 1)
                        dve.wait_ge(zero_done, h + 1)
                    mi = NL if i == 0 else i - 1
                    n = (NL + 1) * h + i
                    need(dve, mask_done, n)
                    carrier(dve)
                    dve.copy_predicated(att[:], masks[:, mi:mi + 1, :].to_broadcast([P, NT, P]),
                                        (s_ps, t_ps)[i % 2][:].rearrange("p (t i) -> p t i", i=P)).then_inc(mask_done, 1)

                def move_values(h, m):
                    f, s = m // 2, m % 2
                    dve.wait_ge(vtr_done, 4 * h + m + 1)
                    if m == 0:
                        need(dve, out_done, 4 * h)
                    dve.tensor_copy(v[:, s * TPS:(s + 1) * TPS, f * P:(f + 1) * P],
                                    v_ps[:].rearrange("p (t e) -> p t e", e=P)).then_inc(v_ready, 1)

                def carry(h, r):
                    s, i = r // ST, r % ST
                    src = (o_ps, v_ps)[r % 2]
                    dve.wait_ge(st_mm, 2 * ST * h + r + 1)
                    if r == 0:
                        dve.wait_ge(dec_done, h + 1)
                    if r > 0:
                        dve.wait_ge(st_done, 2 * ST * h + r)
                    for d in range(2):
                        add = src[:, d * GDV:(d + 1) * GDV]
                        t = s * TPS + (i if d == FW else TPS - 1 - i)
                        if i == 0:
                            ins = dve.tensor_copy(S[:, d, s, 0, :], add)
                        else:
                            ins = dve.scalar_tensor_tensor(out=S[:, d, s, i, :], in0=S[:, d, s, i - 1, :],
                                                           scalar=dec[:, d, t:t + 1], in1=add, op0=ALU.mult, op1=ALU.add)
                    ins.then_inc(st_done, 1)

                def finish(h, s):
                    dve.wait_ge(sd_done, 2 * h + s + 1)
                    if s == 0:
                        for b_ in range(NS):
                            dve.wait_ge(z_free[b_], chunk(h, G + 1) + 1)
                    for f in range(2):
                        dve.scalar_tensor_tensor(out=out_sb[:, s, f, :], in0=out_sb[:, s, f, :], scalar=onorm[:, f:f + 1],
                                                 in1=rstd[:], op0=ALU.mult, op1=ALU.mult).then_inc(t_done, 1)
                    for f in range(2):
                        dve.wait_ge(t_done, 4 * h + 2 * s + f + 1)
                        dve.tensor_tensor(gate[:, f, toks(s)], gate[:, f, toks(s)], out_sb[:, s, f, :], ALU.mult)\
                            .then_inc(y_done, 1)

                def rest(h, n):
                    if n == 0:
                        key_operands(h, NL)
                        pick(h, NL - 1)
                        pick(h, NL)
                    if n == 2:
                        for r in range(2):
                            carry(h, r)
                    if n == 3:
                        for r in range(2, 2 * ST):
                            carry(h, r)
                    if n in (6, 7):
                        finish(h, n - 6)

                def head(h, before):
                    for n in range(SLOTS):
                        if n % 2 == 0 and n < 6:
                            split_lo(dve, chunk(h, n // 2) + 1, slot_of(n // 2 + 1))
                        if before is not None:
                            rest(before, n)
                        if n == 2:
                            need(dve, abs_done, 4 * h)
                            dve.tensor_copy(bgh[:], bg[:, :, bass.ds(h, 1)].rearrange("p d o -> p (d o)")).then_inc(bgh_done, 1)
                            dve.wait_ge(bgh_done, h + 1)
                            minima(h, FW)
                            minima(h, BW)
                            log_sums(h, FW)
                        if n == 3:
                            log_sums(h, BW)
                            tile_sums(h)
                        if n == 10:
                            query_decays(h)
                        for e in entries(n - 1):
                            if e < NL:
                                key_operands(h, e)
                        if 6 <= n < 10:
                            move_values(h, n - 6)
                        if n >= 6:
                            pick(h, n - 6)
                        if n % 2 == 0 and n >= 6:
                            split_lo(dve, chunk(h, n // 2) + 1, slot_of(n // 2 + 1))
                        if n == 8:
                            query_exponents(h)
                        for e in entries(n):
                            exponents(h, e)
                dve.wait_ge(c_in, 16 * 2)
                dve.wait_ge(bg_in, 16 * 2)
                dve.memset(e1[:, SH - 1:SH], 0.0)
                split_lo(dve, C_GLA, C_GLA % 2)
                head(0, None)
                with dve.Fori(1, GLA_HEADS) as h:
                    head(h, h - 1)
                for n in range(8):
                    rest(GLA_HEADS - 1, n)
    return stage


_INS = ["x_prompt", "x_sample", "mem_prompt", "mem_sample", "a_ln", "a_win", "a_mln", "a_wmem", "a_wout", "b_ln",
        "b_win", "b_wg_f", "b_bg_f", "b_wg_b", "b_bg_b", "b_onorm", "b_mln", "b_wmem", "b_wout", "lnf"]
_OUTS = ["y_prompt", "y_sample"]


def constants():
    i = np.arange(P)[:, None]
    j = np.arange(P)[None, :]
    bias = np.empty((P, RES, KEYS), np.float32)
    slope = 0.5 / SCALE
    hidden = -1e30 / SCALE
    for r in range(RES):
        for kt in range(RES):
            d = np.abs((RES * i + r) - (RES * j + kt))
            bias[:, r, kt * P:(kt + 1) * P] = np.where(d <= 64, -d * slope, hidden)
        d = np.abs(i - j)
        bias[:, r, SEQ:SEQ + P] = np.where(d <= 64, -d * slope, hidden)
        bias[:, r, SEQ + P:] = np.where(d % 4 == 0, -(d // 4) * slope, hidden)
    masks = np.zeros((P, len(LEVELS) + 1, P), np.uint32)
    for n, m in enumerate(LEVELS):
        masks[:, n, :] = ((i // (2 * m)) == (j // (2 * m))) & ((i // m) != (j // m))
    masks[:, len(LEVELS), :] = i == j
    starts = np.ones((P, TOK), np.float32)
    starts[:, ::P] = 0.0
    return {"c_ident": np.eye(P, dtype=np.float32), "c_bias": bias, "c_masks": masks, "c_starts": starts}


def kernel(**inputs):
    import concourse.bacc as _bacc
    from concourse.bass_utils import run_bass_kernel_spmd as _run

    nc = _bacc.Bacc("TRN2", target_bir_lowering=False, num_devices=1)
    arrays, args = {}, {}
    given = {n: np.ascontiguousarray(inputs[n]) for n in _INS}
    given.update(constants())
    for name, a in given.items():
        arrays[f"in_{name}"] = a
        args[name] = nc.dram_tensor(f"in_{name}", a.shape, mybir.dt.from_np(a.dtype), kind="ExternalInput").ap()
    for name in _OUTS:
        args[name] = nc.dram_tensor(f"out_{name}", (1, SEQ, D), F32, kind="ExternalOutput").ap()
    build(nc, args)
    r = _run(nc, [arrays], core_ids=[0])
    return tuple(r.results[0][f"out_{name}"] for name in _OUTS)
```
